# Optimizing a Trainium2 kernel written in Bass

```python
import jax, jax.numpy as jnp
from jax import lax
import numpy as np

D_MODEL = 1024
BATCH = 1
SEQ = 256
DEPTH = 1

MIX_WIDTH = D_MODEL
ATT_HEADS = 8
ATT_HEAD_DIM = 64
IDX_HEADS = 8
IDX_DIM = 64
TOPK_MAX = 256
RET_HEADS = 4
RET_QK_DIM = 128
RET_V_DIM = 128
ROPE_THETA = 10000.0
Q_BLOCK = 128
RET_CHUNK = 128
PEER_HEADS = 8
PEER_NKEYS = 128
PEER_KEY_DIM = 256
PEER_HALF = PEER_KEY_DIM // 2
PEER_TOPK = 16
N_EXPERTS = PEER_NKEYS * PEER_NKEYS
N_MOD = 6
EPS = 1e-6

IN_SPLITS = (ATT_HEADS * ATT_HEAD_DIM, ATT_HEADS * ATT_HEAD_DIM, ATT_HEADS * ATT_HEAD_DIM,
             IDX_HEADS * IDX_DIM, IDX_DIM, IDX_HEADS,
             RET_HEADS * RET_QK_DIM, RET_HEADS * RET_QK_DIM, RET_HEADS * RET_V_DIM, RET_HEADS * RET_V_DIM)
IN_COLS = (3 * ATT_HEADS * ATT_HEAD_DIM + IDX_HEADS * IDX_DIM + IDX_DIM + IDX_HEADS
           + 2 * RET_HEADS * RET_QK_DIM + 2 * RET_HEADS * RET_V_DIM)

kernel_name = "hymba_dsa_retnet_peer_adaln"

def rmsnorm(x, g):
    xf = x.astype(jnp.float32)
    y = xf * lax.rsqrt(jnp.mean(xf * xf, axis=-1, keepdims=True) + EPS)
    return (y * g.astype(jnp.float32)).astype(x.dtype)

def rope_inv_freq(d):
    return 1.0 / (ROPE_THETA ** (jnp.arange(0, d, 2, dtype=jnp.float32) / d))

def retnet_inv_freq(d):
    return 1.0 / (ROPE_THETA ** jnp.linspace(0.0, 1.0, d // 2, dtype=jnp.float32))

def rotate(x, inv_freq):
    s = x.shape[1]
    ang = jnp.arange(s, dtype=jnp.float32)[:, None] * inv_freq[None, :]
    cos = jnp.cos(ang)[None, :, None, :]
    sin = jnp.sin(ang)[None, :, None, :]
    x1, x2 = jnp.split(x.astype(jnp.float32), 2, axis=-1)
    return jnp.concatenate([x1 * cos - x2 * sin, x1 * sin + x2 * cos], axis=-1).astype(x.dtype)

def dsa_attention(q, k, v, qi, ki, wi):
    b, s, h, dh = q.shape
    topk = min(TOPK_MAX, s // 4)
    n_blocks = s // Q_BLOCK
    scale = dh ** -0.5
    idx_scale = IDX_DIM ** -0.5
    spos = jnp.arange(s)

    def block(i):
        t0 = i * Q_BLOCK
        qb = lax.dynamic_slice_in_dim(q, t0, Q_BLOCK, axis=1)
        qib = lax.dynamic_slice_in_dim(qi, t0, Q_BLOCK, axis=1)
        wib = lax.dynamic_slice_in_dim(wi, t0, Q_BLOCK, axis=1)
        tpos = t0 + jnp.arange(Q_BLOCK)
        causal = spos[None, :] <= tpos[:, None]
        sc = jnp.einsum('bqhd,bsd->bqhs', qib, ki, preferred_element_type=jnp.float32) * idx_scale
        iscore = jnp.einsum('bqh,bqhs->bqs', wib.astype(jnp.float32), jax.nn.relu(sc))
        iscore = jnp.where(causal[None], iscore, -jnp.inf)
        _, sel = lax.top_k(iscore, topk)
        valid = sel <= tpos[None, :, None]
        kg = jax.vmap(lambda kb, ib: kb[ib])(k, sel)
        vg = jax.vmap(lambda vb, ib: vb[ib])(v, sel)
        logits = jnp.einsum('bqhd,bqkhd->bhqk', qb, kg, preferred_element_type=jnp.float32) * scale
        logits = jnp.where(valid[:, None], logits, -jnp.inf)
        p = jax.nn.softmax(logits, axis=-1)
        return jnp.einsum('bhqk,bqkhd->bqhd', p.astype(v.dtype), vg)

    out = lax.map(block, jnp.arange(n_blocks))
    return out.transpose(1, 0, 2, 3, 4).reshape(b, s, h * dh)

def retention_group(qr, kr, vr, gr):
    b, s, _ = qr.shape
    hh, dk, dv, cl = RET_HEADS, RET_QK_DIM, RET_V_DIM, RET_CHUNK
    n = s // cl
    f32 = jnp.float32
    inv = retnet_inv_freq(dk)
    q = rotate(qr.reshape(b, s, hh, dk), inv).astype(f32)
    k = rotate(kr.reshape(b, s, hh, dk), inv).astype(f32) * (dk ** -0.5)
    v = vr.reshape(b, s, hh, dv).astype(f32)

    def to_chunks(t):
        return t.reshape(b, n, cl, hh, t.shape[-1]).transpose(1, 0, 3, 2, 4)

    qc, kc, vc = to_chunks(q), to_chunks(k), to_chunks(v)
    log_g = jnp.log(1.0 - 2.0 ** (-5.0 - jnp.arange(hh, dtype=f32)))
    idx = jnp.arange(cl)
    diff = (idx[:, None] - idx[None, :]).astype(f32)
    dmat = jnp.where(diff >= 0, jnp.exp(log_g[:, None, None] * jnp.maximum(diff, 0.0)), 0.0)
    xi = jnp.exp(log_g[:, None] * (idx + 1).astype(f32))[None, :, :, None]
    zeta = jnp.exp(log_g[:, None] * (cl - 1 - idx).astype(f32))[None, :, :, None]
    g_chunk = jnp.exp(log_g * cl)[None, :, None, None]

    def step(state, inp):
        qi, ki, vi = inp
        inner = jnp.einsum('bhid,bhjd->bhij', qi, ki) * dmat[None]
        o = (jnp.einsum('bhij,bhjv->bhiv', inner, vi)
             + jnp.einsum('bhid,bhdv->bhiv', qi, state) * xi)
        state = g_chunk * state + jnp.einsum('bhjd,bhjv->bhdv', ki * zeta, vi)
        return state, o

    state0 = jnp.zeros((b, hh, dk, dv), f32)
    _, o = lax.scan(step, state0, (qc, kc, vc))
    o = o.transpose(1, 0, 3, 2, 4).reshape(b, s, hh, dv)
    mu = jnp.mean(o, axis=-1, keepdims=True)
    var = jnp.mean(jnp.square(o - mu), axis=-1, keepdims=True)
    o = ((o - mu) * lax.rsqrt(var + EPS)).reshape(b, s, hh * dv)
    return (jax.nn.silu(gr.astype(f32)) * o).astype(gr.dtype)

def peer_ffn(h, w_pq, sub_keys, u_emb, v_emb):
    b, s, d = h.shape
    nb = s // Q_BLOCK
    t = b * Q_BLOCK
    kk = PEER_TOPK
    hb = h.reshape(b, nb, Q_BLOCK, d).transpose(1, 0, 2, 3).reshape(nb, t, d)

    def block(xb):
        qry = (xb @ w_pq).reshape(t, PEER_HEADS, 2, PEER_HALF)
        sc = jnp.einsum('thpd,hpnd->thpn', qry, sub_keys, preferred_element_type=jnp.float32)
        v1, i1 = lax.top_k(sc[:, :, 0], kk)
        v2, i2 = lax.top_k(sc[:, :, 1], kk)
        cand = (v1[..., :, None] + v2[..., None, :]).reshape(t, PEER_HEADS, kk * kk)
        cid = (i1[..., :, None] * PEER_NKEYS + i2[..., None, :]).reshape(t, PEER_HEADS, kk * kk)
        top_s, pos = lax.top_k(cand, kk)
        eid = jnp.take_along_axis(cid, pos, axis=-1)
        gate = jax.nn.softmax(top_s, axis=-1)
        u = u_emb[eid]
        act = jax.nn.gelu(jnp.einsum('thkd,td->thk', u, xb, preferred_element_type=jnp.float32),
                          approximate=False)
        vv = v_emb[eid]
        return jnp.einsum('thk,thkd->td', (gate * act).astype(xb.dtype), vv)

    out = lax.map(block, hb)
    return out.reshape(nb, b, Q_BLOCK, d).transpose(1, 0, 2, 3).reshape(b, s, d)

def setup_inputs(seed: int = 0) -> dict:
    key = jax.random.key(seed)
    ks = jax.random.split(key, 13)
    f = jnp.float32
    d = D_MODEL
    nrm = jax.random.normal
    return {
        "x": nrm(ks[0], (BATCH, SEQ, d), f),
        "c": nrm(ks[1], (BATCH, d), f),
        "w_ada": nrm(ks[2], (DEPTH, d, N_MOD * d), f) * (0.5 * d ** -0.5),
        "b_ada": 0.01 * nrm(ks[3], (DEPTH, N_MOD * d), f),
        "norm_mix_g": 1.0 + 0.01 * nrm(ks[4], (DEPTH, d), f),
        "w_in": nrm(ks[5], (DEPTH, d, IN_COLS), f) * d ** -0.5,
        "w_out": nrm(ks[6], (DEPTH, MIX_WIDTH, d), f) * MIX_WIDTH ** -0.5,
        "norm_ffn_g": 1.0 + 0.01 * nrm(ks[7], (DEPTH, d), f),
        "w_pq": nrm(ks[8], (DEPTH, d, PEER_HEADS * PEER_KEY_DIM), f) * d ** -0.5,
        "sub_keys": nrm(ks[9], (DEPTH, PEER_HEADS, 2, PEER_NKEYS, PEER_HALF), f) * PEER_HALF ** -0.5,
        "u_emb": nrm(ks[10], (DEPTH, N_EXPERTS, d), f) * d ** -0.5,
        "v_emb": nrm(ks[11], (DEPTH, N_EXPERTS, d), f) * PEER_HEADS ** -0.5,
        "norm_final_g": 1.0 + 0.01 * nrm(ks[12], (d,), f),
    }

def reference(x, c, w_ada, b_ada, norm_mix_g, w_in, w_out, norm_ffn_g, w_pq, sub_keys, u_emb, v_emb,
              norm_final_g):
    b, s, _ = x.shape
    split_pts = tuple(int(p) for p in np.cumsum(np.array(IN_SPLITS))[:-1])
    rope_att = rope_inv_freq(ATT_HEAD_DIM)
    rope_idx = rope_inv_freq(IDX_DIM)
    for layer in range(DEPTH):
        mod = jax.nn.silu(c) @ w_ada[layer] + b_ada[layer]
        sh_m, sc_m, gt_m, sh_f, sc_f, gt_f = jnp.split(mod[:, None, :], N_MOD, axis=-1)

        h = rmsnorm(x, norm_mix_g[layer]) * (1 + sc_m) + sh_m
        proj = h @ w_in[layer]
        qa, ka, va, qi, ki, wi, qr, kr, vr, gr = jnp.split(proj, split_pts, axis=-1)
        qa = rotate(qa.reshape(b, s, ATT_HEADS, ATT_HEAD_DIM), rope_att)
        ka = rotate(ka.reshape(b, s, ATT_HEADS, ATT_HEAD_DIM), rope_att)
        va = va.reshape(b, s, ATT_HEADS, ATT_HEAD_DIM)
        qi = rotate(qi.reshape(b, s, IDX_HEADS, IDX_DIM), rope_idx)
        ki = rotate(ki.reshape(b, s, 1, IDX_DIM), rope_idx)[:, :, 0]
        wi = wi * (IDX_HEADS ** -0.5)
        att = dsa_attention(qa, ka, va, qi, ki, wi)
        ret = retention_group(qr, kr, vr, gr)
        mixed = jnp.concatenate([att, ret.astype(att.dtype)], axis=-1) @ w_out[layer]
        x = x + gt_m * mixed

        h = rmsnorm(x, norm_ffn_g[layer]) * (1 + sc_f) + sh_f
        x = x + gt_f * peer_ffn(h, w_pq[layer], sub_keys[layer], u_emb[layer], v_emb[layer])
    return rmsnorm(x, norm_final_g)


_drawn_inputs = setup_inputs


def setup_inputs(seed=0):
    import zlib

    import numpy as np

    out = dict(_drawn_inputs(seed))
    spreads = {}
    factors = {'b_ada': 4.701, 'norm_mix_g': 8.0, 'norm_ffn_g': 26.604, 'norm_final_g': 33.309}
    for name, (base, spread) in spreads.items():
        noise = np.random.default_rng([zlib.crc32(name.encode()), seed]).standard_normal(out[name].shape)
        drawn = base * np.exp(spread * noise) if base else spread * noise
        out[name] = __import__('jax').numpy.asarray(drawn.astype(out[name].dtype))
    for name, factor in factors.items():
        out[name] = (out[name] * factor).astype(out[name].dtype)
    return out
```

```python
from contextlib import ExitStack

import numpy as np

import concourse.bass as bass
from concourse import mybir

F32 = mybir.dt.float32
F32R = mybir.dt.float32r
U32 = mybir.dt.uint32
ALU = mybir.AluOpType
ACT = mybir.ActivationFunctionType
AX_X = mybir.AxisListType.X

P = 128
D = 1024
KC = D // P
T = 256
TH = T // P
ATT_H, ATT_D = 8, 64
RET_H, RET_D = 4, 128
TOPK = min(256, T // 4)
PEER_H, NKEYS, PTOP = 8, 128, 16
EPS = 1e-6
N_MOD = 6
U_PICK = 2 * PEER_H
PICK_LINKS = 12
DECODE_LINKS = 9
HK = PEER_H * PTOP
DECODE_FROM = 108
U_DECODED = DECODE_FROM // 4

ROT = "rotate"
ROWS = "rows"
GATE = "gate"
PAIRS = [("ki", ROT, 2), ("qi0", ROT, 2), ("qi1", ROT, 2), ("wi", ROWS, 1),
         ("ka0", ROT, 2), ("ka1", ROT, 2), ("qa0", ROT, 2), ("qa1", ROT, 2),
         ("va0", ROWS, 2), ("va1", ROWS, 2),
         ("kr0", ROT, 2), ("kr1", ROT, 2), ("qr0", ROT, 2), ("qr1", ROT, 2),
         ("vr0", ROWS, 2), ("vr1", ROWS, 2), ("gr0", GATE, 2), ("gr1", GATE, 2)]
N_IN = sum(p[2] for p in PAIRS)
N_OUT = KC
N_PQ = 2 * PEER_H
FIRST_OUT = N_IN
FIRST_PQ = FIRST_OUT + N_OUT
N_EARLY = FIRST_PQ + N_PQ
FIRST_U = N_EARLY
FIRST_V = FIRST_U + NKEYS
RING = 4
ADA_GROUP = 4
N_ADA = N_MOD * KC
ADA_LOADS = N_ADA // ADA_GROUP
ADA_SLOTS = 2
NEG = -1.0e30
TAKEN = -3.0e38

TAB = dict(att_cs=(0, 512), att_sc=(512, 1024), ret_cs=(1024, 1536), ret_sc=(1536, 2048),
           decay=(2048, 3072), causal=(3072, 3200))
TAB_W = 3200


def build(nc, xT, cb, ada, ada_b, gains, tables, keep, early, skeys, uw, vw, outT):
    with ExitStack() as ctx:
        def sb(name, shape, dt=F32):
            return ctx.enter_context(nc.sbuf_tensor(name, shape, dt))

        def sem(name):
            return ctx.enter_context(nc.semaphore(name))

        act = sb("act", [P, NKEYS * T])
        h_hi = sb("h_hi", [P, KC, T], F32R)
        h_lo = sb("h_lo", [P, KC, T], F32R)
        x = sb("x", [P, KC, T])
        raw = [sb(f"raw{s}", [P, KC * P]) for s in range(RING)]
        w_hi = [sb(f"w_hi{s}", [P, KC, P], F32R) for s in range(RING)]
        w_lo = [sb(f"w_lo{s}", [P, KC, P], F32R) for s in range(RING)]
        kept = sb("kept", [P, 3, P])
        iota, ident, mean_w = kept[:, 0, :], kept[:, 1, :], kept[:, 2, :]
        hot_l = [sb(f"hot_l{s}", [P, P]) for s in range(2)]
        hot_r = [sb(f"hot_r{s}", [P, P]) for s in range(2)]
        sel = sb("sel", [P, 3, T])
        mod = sb("mod", [P, N_ADA])
        mod_b = sb("mod_b", [P, N_ADA])
        gain = sb("gain", [P, 3, KC])
        gmod = sb("gmod", [P, 2, KC])
        gsum = sb("gsum", [P, TH * PEER_H])

        top = [0]

        def scratch(*dims, at=None):
            n = int(np.prod(dims))
            if at is None:
                at = top[0]
                top[0] += n
            assert at + n <= NKEYS * T, (at, n)
            v = act[:, at:at + n]
            if len(dims) == 2:
                v = v.rearrange("p (a b) -> p a b", a=dims[0])
            elif len(dims) == 3:
                v = v.rearrange("p (a b c) -> p a b c", a=dims[0], b=dims[1])
            return v

        ada_ring = scratch(ADA_SLOTS, ADA_GROUP, D)
        c_row = scratch(D)
        c_tmp = scratch(D)
        tab = scratch(TAB_W)
        rot_a = scratch(2, T)
        rot_b = scratch(2, T)
        ka = scratch(2, 2, T)
        qa = scratch(2, 2, T)
        qi = scratch(2, 2, T)
        ki = scratch(2, T)
        kr = scratch(2, 2, T)
        qr = scratch(2, 2, T)
        gr = scratch(4, T)
        va = scratch(TH, 512)
        vr = scratch(TH, 512)
        wi = scratch(TH, 8)
        isc = scratch(TH, T)
        best = scratch(8)
        mask = scratch(TH, T)
        inner = scratch(RET_H, 384)
        rmax = scratch(8)
        rsum = scratch(8)
        rinv = scratch(8)
        shared = top[0]
        norm_fin = scratch(KC, T, at=0)
        norm_a = scratch(KC, T, at=shared)
        norm_b = scratch(KC, T, at=shared + 2048)
        relu = scratch(8, T, at=shared)
        prob = scratch(8, T, at=shared)
        probT = scratch(2, 8, P, at=shared + 2048)
        rstd = scratch(T, at=shared + 4096)
        ro = scratch(4, T, at=shared + 4096 + 256)
        rsq = scratch(4, T, at=shared + 5120 + 256)
        print_top = shared + 6400
        assert print_top <= NKEYS * T, print_top
        top[0] = NKEYS * T // 2
        qry = scratch(2 * PEER_H, T)
        sk = scratch(2 * PEER_H, NKEYS)
        score = scratch(TH, PEER_H, 2 * NKEYS)
        wk = scratch(2, NKEYS)
        val = scratch(2, PTOP)
        idx = scratch(2, PTOP)
        cand = scratch(PTOP, PTOP)
        cval = scratch(PTOP)
        cpos = scratch(PTOP)
        assert top[0] <= DECODE_FROM * T
        top[0] = DECODE_FROM * T
        top_p = scratch(TH, HK)
        key1 = scratch(TH, HK)
        key2 = scratch(TH, HK)
        rank_u = scratch(HK)
        rank_f = scratch(2, HK)
        hit = scratch(HK, PTOP)
        assert top[0] <= NKEYS * T, top[0]

        def u32(ap):
            return ap.bitcast(U32)

        def tb(name):
            return tab[:, TAB[name][0]:TAB[name][1]]

        ps = ctx.enter_context(nc.psum_tensor("ps", [P, 8, 512], F32))

        x_loaded = sem("x_loaded")
        c_loaded = sem("c_loaded")
        small_loaded = sem("small_loaded")
        tab_loaded = sem("tab_loaded")
        kept_loaded = sem("kept_loaded")
        sk_loaded = sem("sk_loaded")
        ada_loaded = [sem(f"ada_loaded{s}") for s in range(ADA_SLOTS)]
        raw_loaded = [sem(f"raw_loaded{s}") for s in range(RING)]
        hi_ready = sem("hi_ready")
        lo_ready = sem("lo_ready")
        block_used = sem("block_used")
        c_ready = sem("c_ready")
        c_exp = sem("c_exp")
        ada_used = sem("ada_used")
        squares = sem("squares")
        mean_ready = sem("mean_ready")
        mean_eps = sem("mean_eps")
        root_ready = sem("root_ready")
        normed = sem("normed")
        affine = sem("affine")
        h_hi_ready = sem("h_hi_ready")
        h_ready = sem("h_ready")
        chain = sem("chain")
        evac_v = sem("evac_v")
        evac_s = sem("evac_s")
        gate_exp = sem("gate_exp")
        isc_ready = sem("isc_ready")
        relu_ready = sem("relu_ready")
        relu_used = sem("relu_used")
        logit_ready = sem("logit_ready")
        logit_used = sem("logit_used")
        shifted = sem("shifted")
        exp_ready = sem("exp_ready")
        prob_ready = sem("prob_ready")
        probT_ready = sem("probT_ready")
        probT_copied = sem("probT_copied")
        att_ready = sem("att_ready")
        mix_hi = sem("mix_hi")
        att_split = sem("att_split")
        inner_ready = sem("inner_ready")
        inner_used = sem("inner_used")
        ret_ready = sem("ret_ready")
        ret_copied = sem("ret_copied")
        gmean_ready = sem("gmean_ready")
        centred = sem("centred")
        gvar_ready = sem("gvar_ready")
        gvar_eps = sem("gvar_eps")
        groot = sem("groot")
        ret_done = sem("ret_done")
        ret_hi = sem("ret_hi")
        mix_ready = sem("mix_ready")
        out_added = sem("out_added")
        qry_copied = sem("qry_copied")
        score_ready = sem("score_ready")
        score_copied = sem("score_copied")
        gelu_ready = sem("gelu_ready")
        searches = sem("searches")
        picked = sem("picked")
        decoded = sem("decoded")
        pick_exp = sem("pick_exp")
        sel_rows = sem("sel_rows")
        sel_T = sem("sel_T")
        sel_ready = sem("sel_ready")
        hot_ready = sem("hot_ready")
        hot_used = sem("hot_used")
        gates_used = sem("gates_used")
        wexp_hi = sem("wexp_hi")
        wexp_lo = sem("wexp_lo")
        out_ready = sem("out_ready")
        stored = sem("stored")

        block = ctx.enter_context(nc.Block())

        evac = []
        nv = ns = 0
        for _, kind, _ in PAIRS:
            if kind == ROWS:
                ns += 1
                evac.append((evac_s, ns))
            else:
                nv += 1
                evac.append((evac_v, nv))
        n_evac_v, n_evac_s = nv, ns
        pair_of, half_of, last_of = [], [], []
        for q, (_, _, blocks) in enumerate(PAIRS):
            for i in range(blocks):
                pair_of.append(q)
                half_of.append(i)
            last_of.append(len(pair_of) - 1)

        def proj_bank(q):
            return ps[:, q % 4, :]

        @block.sync
        def _(sp):
            sp.dma_start(x[:], xT).then_inc(x_loaded, 16)
            sp.dma_start(kept[:], keep).then_inc(kept_loaded, 16)
            sp.dma_start(tab, tables).then_inc(tab_loaded, 16)

            def load(source, slot):
                sp.dma_start(raw[slot][:], source).then_inc(raw_loaded[slot], 16)

            for n in range(RING):
                load(early[n], n)
            rounds = N_EARLY // RING
            with sp.Fori(1, rounds) as i:
                for s in range(RING):
                    sp.wait_ge(lo_ready, i * RING + s - RING + 1)
                    sp.dma_start(raw[s][:], early[bass.ds(i * RING + s, 1)].rearrange("a p n -> (a p) n")
                                 ).then_inc(raw_loaded[s], 16)
            for n in range(rounds * RING, N_EARLY):
                sp.wait_ge(lo_ready, n - RING + 1)
                load(early[n], n % RING)
            sp.wait_ge(out_added, KC)
            sp.dma_start(sk, skeys).then_inc(sk_loaded, 16)
            for first, source in ((FIRST_U, uw), (FIRST_V, vw)):
                with sp.Fori(0, NKEYS // RING) as i:
                    for j in range(RING):
                        s = (first + j) % RING
                        sp.wait_ge(lo_ready, i * RING + (first + j - RING + 1))
                        sp.dma_start(raw[s][:], source[bass.ds(i * RING + j, 1)].rearrange("a p n -> (a p) n")
                                     ).then_inc(raw_loaded[s], 16)
            for c in range(2):
                sp.wait_ge(out_ready, c + 1)
                sp.dma_start(outT[:, c * KC // 2:(c + 1) * KC // 2, :],
                             norm_fin[:, c * KC // 2:(c + 1) * KC // 2, :]).then_inc(stored, 16)
            sp.wait_ge(stored, 32)

        @block.gpsimd
        def _(pool):
            pool.dma_start(c_row, cb).then_inc(c_loaded, 16)
            pool.dma_start(mod_b[:], ada_b).then_inc(small_loaded, 16)
            pool.dma_start(gain[:], gains).then_inc(small_loaded, 16)
            for n in range(ADA_LOADS):
                if n >= ADA_SLOTS:
                    pool.wait_ge(ada_used, (n - ADA_SLOTS + 1) * ADA_GROUP)
                pool.dma_start(ada_ring[:, n % ADA_SLOTS].rearrange("p g k -> p (g k)"), ada[n]).then_inc(ada_loaded[n % ADA_SLOTS], 16)

        @block.scalar
        def _(e):
            def split_hi(n, slot, turn):
                e.wait_ge(raw_loaded[slot], turn * 16)
                if not isinstance(n, int) or n >= RING:
                    e.wait_ge(block_used, n - RING + 1)
                e.activation(w_hi[slot][:], raw[slot][:].rearrange("p (k m) -> p k m", k=KC),
                             ACT.Copy).then_inc(hi_ready, 1)

            def norm(i):
                e.wait_ge(mean_eps, i + 1)
                e.activation(rstd, rstd, ACT.Sqrt).then_inc(root_ready, 1)
                if i == 2:
                    return
                e.wait_ge(normed, i + 1)
                for k in range(KC):
                    e.activation(norm_b[:, k, :], norm_a[:, k, :], ACT.Identity, scale=gmod[:, i, k:k + 1],
                                 bias=mod[:, (0 if i == 0 else 3 * KC) + k:(0 if i == 0 else 3 * KC) + k + 1]
                                 ).then_inc(affine, 1)
                e.wait_ge(affine, (i + 1) * KC)
                e.activation(h_hi[:], norm_b, ACT.Copy).then_inc(h_hi_ready, 1)

            e.wait_ge(c_loaded, 16)
            e.activation(c_tmp, c_row, ACT.Exp, scale=-1.0).then_inc(c_exp, 1)
            for n in range(RING):
                split_hi(n, n, 1)
            norm(0)
            gates = 0

            def take(q):
                nonlocal gates
                name, kind, _ = PAIRS[q]
                e.wait_ge(block_used, last_of[q] + 1)
                src = proj_bank(q)
                if kind == GATE:
                    i = int(name[-1])
                    e.activation(gr[:, 2 * i:2 * i + 2, :], src.rearrange("p (a b) -> p a b", a=2), ACT.Exp,
                                 scale=-1.0).then_inc(gate_exp, 1)
                elif name == "wi":
                    e.activation(wi, src[:, 0:256].rearrange("p (a b) -> p a b", a=2)[:, :, 0:8], ACT.Copy,
                                 scale=float(ATT_H) ** -0.5).then_inc(evac_s, 1)
                else:
                    i = int(name[-1])
                    dst = (va if name[1] == "a" else vr)[:, :, 256 * i:256 * i + 256]
                    e.activation(dst.rearrange("p t (b c) -> p b t c", b=2),
                                 src.rearrange("p (b t c) -> p b t c", b=2, t=2), ACT.Copy).then_inc(evac_s, 1)

            def index_relu(b):
                S = P * (b + 1)
                e.wait_ge(isc_ready, b + 1)
                if b:
                    e.wait_ge(relu_used, b)
                for g in range(4):
                    e.activation(relu[:, 2 * g:2 * g + 2, 0:S],
                                 ps[:, 4 + g, :].rearrange("p (a s) -> p a s", a=2)[:, :, 0:S], ACT.Relu,
                                 scale=0.125).then_inc(relu_ready, 1)

            for n in range(RING, N_IN + RING):
                split_hi(n, n % RING, n // RING + 1)
                if n - 3 < N_IN and n - 3 == last_of[pair_of[n - 3]] and PAIRS[pair_of[n - 3]][1] != ROT:
                    take(pair_of[n - 3])
                if n == 18:
                    index_relu(0)
                if n == 22:
                    index_relu(1)
            e.wait_ge(ret_ready, 1)
            e.activation(ro, ps[:, 0:2, :].rearrange("p a (b t) -> p (a b) t", b=2), ACT.Copy).then_inc(ret_copied, 1)
            e.wait_ge(gvar_eps, 1)
            e.activation(rsq, rsq, ACT.Sqrt).then_inc(groot, 1)
            e.wait_ge(ret_done, 1)
            e.activation(h_hi[:, 4:8, :], ro, ACT.Copy).then_inc(ret_hi, 1)
            for b in range(TH):
                S = P * (b + 1)
                e.wait_ge(shifted, b + 1)
                for h in range(8):
                    e.activation(prob[:, h, 0:S], prob[:, h, 0:S], ACT.Exp, bias=rmax[:, h:h + 1],
                                 accum_out=rsum[:, h:h + 1]).then_inc(exp_ready, 1)
                e.wait_ge(probT_ready, b + 1)
                for ck in range(b + 1):
                    e.activation(probT[:, ck].rearrange("p (a h) t -> p a h t", a=2),
                                 ps[:, 2 * ck:2 * ck + 2, :].rearrange("p a (h t) -> p a h t", h=4), ACT.Copy
                                 ).then_inc(probT_copied, 1)
                e.wait_ge(att_ready, b + 1)
                e.activation(h_hi[:, 0:4, P * b:P * b + P],
                             ps[:, 4, :].rearrange("p (a t) -> p a t", a=4), ACT.Copy).then_inc(mix_hi, 1)
            for n in range(FIRST_OUT + RING, FIRST_PQ):
                split_hi(n, n % RING, n // RING + 1)
            for n in range(FIRST_PQ, FIRST_PQ + RING):
                split_hi(n, n % RING, n // RING + 1)
            norm(1)

            def take_query(i):
                e.wait_ge(block_used, FIRST_PQ + i + 1)
                e.activation(qry[:, i, :], ps[:, i % 4, 0:T], ACT.Copy).then_inc(qry_copied, 1)

            for n in range(FIRST_PQ + RING, N_EARLY):
                split_hi(n, n % RING, n // RING + 1)
                take_query(n - FIRST_PQ - RING)
            for i in range(N_PQ - RING, N_PQ):
                take_query(i)
            for b in range(TH):
                e.wait_ge(score_ready, b + 1)
                e.activation(score[:, b].rearrange("p (a h) n -> p a (h n)", a=4), ps[:, 4:8, :],
                             ACT.Copy).then_inc(score_copied, 1)
            e.preload_act_table(ACT.Gelu)

            def gelu(n, i2, bank):
                e.wait_ge(block_used, n + 1)
                e.activation(act[:, bass.ds(i2 * T, T)], ps[:, bank, 0:T], ACT.Gelu).then_inc(gelu_ready, 1)

            def experts(a, z):
                with e.Fori(a, z) as i:
                    for j in range(RING):
                        n = FIRST_U + RING + j
                        split_hi(i * RING + n, n % RING, i + (n // RING + 1))
                        gelu(i * RING + (FIRST_U + j), i * RING + j, j)

            for j in range(RING):
                n = FIRST_U + j
                split_hi(n, n % RING, n // RING + 1)
            experts(0, U_PICK)
            e.wait_ge(picked, U_PICK)
            experts(U_PICK, U_DECODED)
            e.wait_ge(decoded, TH)
            experts(U_DECODED, NKEYS // RING - 1)
            for j in range(RING):
                n = FIRST_V + j
                split_hi(n, n % RING, n // RING + 1)
                gelu(FIRST_V - RING + j, NKEYS - RING + j, j)
            e.activation(sel[:, 2, :], sel[:, 2, :], ACT.Exp).then_inc(pick_exp, 1)

            def expert_hi(i2, slot):
                e.activation(h_hi[:, slot, :], act[:, bass.ds(i2 * T, T)], ACT.Copy).then_inc(wexp_hi, 1)

            e.wait_ge(gates_used, T // 4)
            for j in range(RING):
                expert_hi(j, j)
            with e.Fori(0, NKEYS // RING - 1) as i:
                for j in range(RING):
                    n = FIRST_V + RING + j
                    split_hi(i * RING + n, n % RING, i + (n // RING + 1))
                    expert_hi(i * RING + (RING + j), j)
            norm(2)

        @block.vector
        def _(e):
            base, steps = [0], [0]

            def link(ins, search=False):
                steps[0] += 1
                ins.then_inc(chain, 1)
                e.wait_ge(chain, base[0] + steps[0])
                if search:
                    e.sem_inc(searches, 1)

            def split_lo(n, slot):
                e.wait_ge(hi_ready, n + 1)
                e.tensor_tensor(w_lo[slot][:], raw[slot][:].rearrange("p (k m) -> p k m", k=KC),
                                w_hi[slot][:].bitcast(F32), ALU.subtract).then_inc(lo_ready, 1)

            def ada_blocks(a, b):
                for m in range(a, b):
                    load = m // ADA_GROUP
                    e.wait_ge(ada_loaded[load % ADA_SLOTS], 16 * (load // ADA_SLOTS + 1))
                    w = ada_ring[:, load % ADA_SLOTS, m % ADA_GROUP, :]
                    e.tensor_tensor_reduce(w, w, c_row, 1.0, 0.0, ALU.mult, ALU.add,
                                           mod[:, m:m + 1]).then_inc(ada_used, 1)
                e.wait_ge(ada_used, b)
                link(e.tensor_tensor(mod[:, a:b], mod[:, a:b], mod_b[:, a:b], ALU.add))

            def gain_mod(i):
                a = KC if i == 0 else 4 * KC
                link(e.scalar_tensor_tensor(out=gmod[:, i, :], in0=mod[:, a:a + KC], scalar=1.0,
                                            in1=gain[:, i, :], op0=ALU.add, op1=ALU.mult))

            def norm(i):
                e.tensor_tensor(norm_a, x[:], x[:], ALU.mult).then_inc(squares, 1)
                e.wait_ge(mean_ready, i + 1)
                e.tensor_scalar(rstd, ps[:, 7, 0:T], 1.0 / KC, EPS, ALU.mult, ALU.add).then_inc(mean_eps, 1)
                e.wait_ge(root_ready, i + 1)
                link(e.reciprocal(rstd, rstd))

            def norm_in(i):
                norm(i)
                e.tensor_tensor(norm_a, x[:], rstd[:, None, :].to_broadcast([P, KC, T]),
                                ALU.mult).then_inc(normed, 1)
                e.wait_ge(h_hi_ready, i + 1)
                e.tensor_tensor(h_lo[:], norm_b, h_hi[:].bitcast(F32), ALU.subtract).then_inc(h_ready, 1)

            e.wait_ge(c_exp, 1)
            link(e.tensor_scalar(c_tmp, c_tmp, 1.0, None, ALU.add))
            link(e.reciprocal(c_tmp, c_tmp))
            link(e.tensor_tensor(c_row, c_row, c_tmp, ALU.mult))
            e.wait_ge(small_loaded, 32)
            ada_blocks(0, 2 * KC)
            gain_mod(0)
            e.wait_ge(x_loaded, 16)
            for n in range(RING):
                split_lo(n, n)
            norm_in(0)

            dest = dict(ki=(ki,), qi=(qi[:, 0], qi[:, 1]), ka=(ka[:, 0], ka[:, 1]), qa=(qa[:, 0], qa[:, 1]),
                        kr=(kr[:, 0], kr[:, 1]), qr=(qr[:, 0], qr[:, 1]))

            def rotate(q):
                name = PAIRS[q][0]
                out = dest[name[:2]][int(name[2:] or 0)]
                kind = "ret" if name[1] == "r" else "att"
                e.wait_ge(block_used, last_of[q] + 1)
                pair = proj_bank(q)
                e.tensor_tensor(rot_a.rearrange("p a b -> p (a b)"), pair, tb(kind + "_cs"), ALU.mult)
                link(e.tensor_tensor(rot_b.rearrange("p a b -> p (a b)"), pair, tb(kind + "_sc"), ALU.mult))
                e.tensor_tensor(out[:, 0, :], rot_a[:, 0, :], rot_a[:, 1, :], ALU.subtract)
                last = e.tensor_tensor(out[:, 1, :], rot_b[:, 0, :], rot_b[:, 1, :], ALU.add)
                last.then_inc(evac_v, 1)
                e.wait_ge(evac_v, evac[q][1])

            def gate(q):
                i = int(PAIRS[q][0][-1])
                g = gr[:, 2 * i:2 * i + 2, :]
                e.wait_ge(gate_exp, i + 1)
                link(e.tensor_scalar(g, g, 1.0, None, ALU.add))
                link(e.reciprocal(g, g))
                e.tensor_tensor(g, proj_bank(q).rearrange("p (a b) -> p a b", a=2), g, ALU.mult).then_inc(evac_v, 1)
                e.wait_ge(evac_v, evac[q][1])

            def index_sum(b):
                S = P * (b + 1)
                if b == 0:
                    e.wait_ge(evac_s, evac[3][1])
                for k in range(8):
                    g, tile = k // 2, k % 2
                    h = 4 * tile + g
                    e.wait_ge(relu_ready, 4 * b + g + 1)
                    if k == 0:
                        link(e.tensor_scalar(isc[:, b, 0:S], relu[:, k, 0:S], wi[:, b, h:h + 1], None, ALU.mult))
                    else:
                        ins = e.scalar_tensor_tensor(out=isc[:, b, 0:S], in0=relu[:, k, 0:S], scalar=wi[:, b, h:h + 1],
                                                     in1=isc[:, b, 0:S], op0=ALU.mult, op1=ALU.add)
                        if k == 7:
                            ins.then_inc(relu_used, 1)
                            e.wait_ge(relu_used, b + 1)
                        else:
                            link(ins)
                diag = isc[:, b, P * b:P * b + P]
                link(e.tensor_tensor(diag, diag, tb("causal"), ALU.add))

            def index_pick(b, a, z):
                S = P * (b + 1)
                s = isc[:, b, 0:S]
                for _ in range(a, z):
                    link(e.max(best, s))
                    link(e.match_replace(s, best, s, TAKEN))

            def index_mask(b):
                S = P * (b + 1)
                link(e.tensor_scalar(mask[:, b, 0:S], isc[:, b, 0:S], 0.5 * TAKEN, NEG, ALU.is_gt, ALU.mult))
                diag = mask[:, b, P * b:P * b + P]
                link(e.tensor_tensor(diag, diag, tb("causal"), ALU.add))

            e.wait_ge(tab_loaded, 16)
            ada_at = [2 * KC]
            for n in range(RING, N_IN + RING):
                split_lo(n, n % RING)
                if n - 3 < N_IN and n - 3 == last_of[pair_of[n - 3]]:
                    q = pair_of[n - 3]
                    if PAIRS[q][1] == ROT:
                        rotate(q)
                    elif PAIRS[q][1] == GATE:
                        gate(q)
                if n == 19:
                    index_sum(0)
                elif n == 23:
                    index_sum(1)
                elif 20 <= n < 23:
                    index_pick(0, (n - 20) * 3, min(8, (n - 19) * 3))
                elif 24 <= n < 32:
                    index_pick(1, n - 24, n - 23)
                elif ada_at[0] < 3 * KC:
                    ada_blocks(ada_at[0], ada_at[0] + 4)
                    ada_at[0] += 4
            index_mask(0)
            index_mask(1)

            e.wait_ge(inner_ready, 1)
            for r in range(RET_H):
                pr = ps[:, 4 + r, 0:384]
                dec_r = tb("decay").rearrange("p (r t) -> p r t", r=RET_H)[:, r, :]
                e.tensor_tensor(inner[:, r, 0:256], pr[:, 0:256], dec_r, ALU.mult)
                last = e.tensor_tensor(inner[:, r, 256:384], pr[:, 256:384], dec_r[:, 0:P], ALU.mult)
            last.then_inc(inner_used, 1)
            e.wait_ge(inner_used, 1)

            def softmax_in(b):
                S = P * (b + 1)
                e.wait_ge(logit_ready, b + 1)
                m = mask[:, b, 0:S]
                src = ps[:, 4:8, :].rearrange("p g (a s) -> p (g a) s", a=2)[:, :, 0:S]
                e.scalar_tensor_tensor(out=prob[:, :, 0:S], in0=src, scalar=float(ATT_D) ** -0.5,
                                       in1=m[:, None, :].to_broadcast([P, 8, S]), op0=ALU.mult,
                                       op1=ALU.add).then_inc(logit_used, 1)
                e.wait_ge(logit_used, b + 1)
                link(e.tensor_reduce(rmax, prob[:, :, 0:S], AX_X, ALU.max))
                e.tensor_scalar(rmax, rmax, -1.0, None, ALU.mult).then_inc(shifted, 1)

            def softmax_out(b):
                S = P * (b + 1)
                e.wait_ge(exp_ready, 8 * (b + 1))
                link(e.reciprocal(rinv, rsum))
                e.tensor_tensor(prob[:, :, 0:S], prob[:, :, 0:S], rinv[:, :, None].to_broadcast([P, 8, S]),
                                ALU.mult).then_inc(prob_ready, 1)
                e.wait_ge(prob_ready, b + 1)

            e.wait_ge(ret_copied, 1)
            e.wait_ge(gmean_ready, 1)
            flat = ps[:, 2:4, :].rearrange("p a (b t) -> p (a b) t", b=2)
            link(e.tensor_tensor(ro, ro, flat, ALU.subtract))
            e.tensor_tensor(rsq, ro, ro, ALU.mult).then_inc(centred, 1)
            e.wait_ge(gvar_ready, 1)
            e.tensor_scalar(rsq, flat, EPS, None, ALU.add).then_inc(gvar_eps, 1)
            e.wait_ge(groot, 1)
            link(e.reciprocal(rsq, rsq))
            link(e.tensor_tensor(ro, ro, rsq, ALU.mult))
            e.tensor_tensor(ro, ro, gr, ALU.mult).then_inc(ret_done, 1)
            e.wait_ge(ret_hi, 1)
            e.tensor_tensor(h_lo[:, 4:8, :], ro, h_hi[:, 4:8, :].bitcast(F32), ALU.subtract).then_inc(mix_ready, 1)

            for b in range(TH):
                softmax_in(b)
                softmax_out(b)
                e.wait_ge(mix_hi, b + 1)
                cols = slice(P * b, P * b + P)
                e.tensor_tensor(h_lo[:, 0:4, cols], ps[:, 4, :].rearrange("p (a t) -> p a t", a=4),
                                h_hi[:, 0:4, cols].bitcast(F32), ALU.subtract).then_inc(mix_ready, 1)

            def add_out(c):
                e.wait_ge(block_used, FIRST_OUT + c + 1)
                e.scalar_tensor_tensor(out=x[:, c, :], in0=ps[:, c % 4, 0:T], scalar=mod[:, 2 * KC + c:2 * KC + c + 1],
                                       in1=x[:, c, :], op0=ALU.mult, op1=ALU.add).then_inc(out_added, 1)

            for n in range(FIRST_OUT + RING, FIRST_PQ):
                split_lo(n, n % RING)
                add_out(n - FIRST_OUT - RING)
            for n in range(FIRST_PQ, FIRST_PQ + RING):
                split_lo(n, n % RING)
                add_out(n - FIRST_PQ + RING)
            ada_blocks(3 * KC, N_ADA)
            gain_mod(1)
            e.wait_ge(out_added, KC)
            norm_in(1)
            for n in range(FIRST_PQ + RING, N_EARLY):
                split_lo(n, n % RING)

            for j in range(RING):
                split_lo(FIRST_U + j, (FIRST_U + j) % RING)
            e.wait_ge(score_copied, TH)
            start = base[0] + steps[0]
            with e.Fori(0, U_PICK) as i:
                base[0], steps[0] = i * PICK_LINKS + start, 0
                src = score.rearrange("p a h n -> p (a h n)")
                link(e.tensor_copy(wk.rearrange("p a n -> p (a n)"), src[:, bass.ds(i * (2 * NKEYS), 2 * NKEYS)]), search=True)
                for half in range(2):
                    v = [val[:, p, 8 * half:8 * half + 8] for p in range(2)]
                    ix = [idx[:, p, 8 * half:8 * half + 8] for p in range(2)]
                    e.max(v[0], wk[:, 0, :])
                    link(e.max(v[1], wk[:, 1, :]), search=True)
                    e.max_index(u32(ix[0]), v[0], wk[:, 0, :])
                    link(e.max_index(u32(ix[1]), v[1], wk[:, 1, :]), search=(half == 0))
                    if half == 0:
                        e.match_replace(wk[:, 0, :], v[0], wk[:, 0, :], TAKEN)
                        link(e.match_replace(wk[:, 1, :], v[1], wk[:, 1, :], TAKEN))
                    n = FIRST_U + RING + half
                    split_lo(i * RING + n, n % RING)
                link(e.tensor_tensor(cand, val[:, 0, :, None].to_broadcast([P, PTOP, PTOP]),
                                     val[:, 1, None, :].to_broadcast([P, PTOP, PTOP]), ALU.add), search=True)
                c = cand.rearrange("p a b -> p (a b)")
                for half in range(2):
                    v, ix = cval[:, 8 * half:8 * half + 8], cpos[:, 8 * half:8 * half + 8]
                    link(e.max(v, c), search=True)
                    link(e.max_index(u32(ix), v, c), search=(half == 0))
                    if half == 0:
                        link(e.match_replace(c, v, c, TAKEN))
                    n = FIRST_U + RING + 2 + half
                    split_lo(i * RING + n, n % RING)
                at = bass.ds(i * PTOP, PTOP)
                e.tensor_scalar(sel[:, 2, :][:, at], cval, cval[:, 0:1], None, ALU.subtract)
                e.tensor_copy(key1.rearrange("p a n -> p (a n)")[:, at], u32(idx[:, 0, :]))
                e.tensor_copy(key2.rearrange("p a n -> p (a n)")[:, at], u32(idx[:, 1, :]))
                e.tensor_copy(u32(top_p.rearrange("p a n -> p (a n)"))[:, at], u32(cpos)).then_inc(picked, 1)
                e.wait_ge(picked, i + 1)
            assert steps[0] == PICK_LINKS, steps
            base[0], steps[0] = start + U_PICK * PICK_LINKS, 0

            start = base[0]
            with e.Fori(0, TH) as i:
                base[0], steps[0] = i * DECODE_LINKS + start, 0
                at = bass.ds(i * HK, HK)
                pos = u32(top_p.rearrange("p a n -> p (a n)"))[:, at]
                ranks = rank_f
                for w, (keys, op, arg) in enumerate(((key1, ALU.logical_shift_right, 4), (key2, ALU.bitwise_and, 15))):
                    link(e.tensor_scalar(u32(rank_u), pos, arg, None, op))
                    link(e.tensor_copy(ranks[:, w, :], u32(rank_u)))
                blocks = iter(range(3 * RING))

                def next_lo():
                    j = next(blocks)
                    n = FIRST_U + RING * (U_PICK + 1) + j
                    split_lo(i * (3 * RING) + n, n % RING)

                for w, keys in enumerate((key1, key2)):
                    next_lo()
                    link(e.tensor_tensor(hit, iota[:, None, 0:PTOP].to_broadcast([P, HK, PTOP]),
                                         ranks[:, w, :, None].to_broadcast([P, HK, PTOP]), ALU.is_equal))
                    next_lo()
                    next_lo()
                    k4 = keys.rearrange("p a n -> p (a n)")[:, at].rearrange("p (h r) -> p h r", h=PEER_H)
                    h4 = hit.rearrange("p (h k) r -> p h k r", h=PEER_H)
                    link(e.tensor_tensor(h4, h4, k4[:, :, None, :].to_broadcast([P, PEER_H, PTOP, PTOP]), ALU.mult))
                    next_lo()
                    next_lo()
                    ins = e.tensor_reduce(sel[:, w, :][:, at], hit, AX_X, ALU.add)
                    if w:
                        ins.then_inc(decoded, 1)
                        e.wait_ge(decoded, i + 1)
                    else:
                        link(ins)
                    next_lo()
            assert steps[0] == DECODE_LINKS, steps
            base[0], steps[0] = start + TH * DECODE_LINKS, 0
            with e.Fori(U_PICK + 6, NKEYS // RING - 1) as i:
                for j in range(RING):
                    n = FIRST_U + RING + j
                    split_lo(i * RING + n, n % RING)
            for j in range(RING):
                split_lo(FIRST_V + j, (FIRST_V + j) % RING)

            e.wait_ge(pick_exp, 1)
            g3 = sel[:, 2, :].rearrange("p (h k) -> p h k", k=PTOP)
            link(e.tensor_reduce(gsum[:], g3, AX_X, ALU.add))
            link(e.reciprocal(gsum[:], gsum[:]))
            e.tensor_tensor(g3, g3, gsum[:, :, None].to_broadcast([P, TH * PEER_H, PTOP]),
                            ALU.mult).then_inc(sel_rows, 1)
            e.wait_ge(sel_T, 1)
            e.tensor_copy(sel[:, 0:2, :], ps[:, 4, :].rearrange("p (a t) -> p a t", a=2))
            link(e.tensor_copy(sel[:, 2, :], ps[:, 5, 0:T]))

            def hot(t, s, wait):
                if wait:
                    e.wait_ge(hot_used, t - 1)
                e.tensor_scalar(hot_l[s][:], iota, sel[:, 0, :][:, bass.ds(t, 1)], sel[:, 2, :][:, bass.ds(t, 1)],
                                ALU.is_equal, ALU.mult)
                e.tensor_scalar(hot_r[s][:], iota, sel[:, 1, :][:, bass.ds(t, 1)], None,
                                ALU.is_equal).then_inc(hot_ready, 1)

            acts = act[:].rearrange("p (i t) -> p i t", t=T)

            def weigh(g, bank):
                e.wait_ge(hot_used, g * 4 + 4)
                v = acts[:, :, bass.ds(g * 4, 4)]
                e.tensor_tensor(v, ps[:, bank, :].rearrange("p (t i) -> p i t", t=4), v,
                                ALU.mult).then_inc(gates_used, 1)

            for t in range(8):
                hot(t, t % 2, t >= 2)
                if t == 5:
                    weigh(0, 4)
            with e.Fori(1, T // 8) as i:
                for t in range(8):
                    hot(i * 8 + t, t % 2, True)
                    if t == 1:
                        weigh(i * 2 - 1, 5)
                    if t == 5:
                        weigh(i * 2, 4)
            weigh(T // 4 - 1, 5)

            def expert_lo(i2, slot):
                e.wait_ge(wexp_hi, i2 + 1)
                e.tensor_tensor(h_lo[:, slot, :], act[:, bass.ds(i2 * T, T)], h_hi[:, slot, :].bitcast(F32),
                                ALU.subtract).then_inc(wexp_lo, 1)

            for j in range(RING):
                expert_lo(j, j)
            with e.Fori(0, NKEYS // RING - 1) as i:
                for j in range(RING):
                    n = FIRST_V + RING + j
                    split_lo(i * RING + n, n % RING)
                    expert_lo(i * RING + (RING + j), j)
            e.wait_ge(block_used, FIRST_V + NKEYS)
            for c in range(KC):
                ins = e.scalar_tensor_tensor(out=x[:, c, :], in0=ps[:, 4 + c // 2, (c % 2) * T:(c % 2) * T + T],
                                             scalar=mod[:, 5 * KC + c:5 * KC + c + 1], in1=x[:, c, :],
                                             op0=ALU.mult, op1=ALU.add)
            link(ins)
            norm(2)
            for c in range(KC):
                ins = e.scalar_tensor_tensor(out=norm_fin[:, c, :], in0=x[:, c, :], scalar=gain[:, 2, c:c + 1],
                                             in1=rstd, op0=ALU.mult, op1=ALU.mult)
                if c % (KC // 2) == KC // 2 - 1:
                    ins.then_inc(out_ready, 1)

        @block.tensor
        def _(e):
            def product(out, a, b, start, stop, check=True):
                (a_hi, a_lo), (b_hi, b_lo) = a, b
                e.matmul(out, a_hi, b_hi, start=start, stop=False, skip_group_check=not check)
                e.matmul(out, a_hi, b_lo, start=False, stop=False, skip_group_check=not check)
                return e.matmul(out, a_lo, b_hi, start=False, stop=stop, skip_group_check=not check)

            def columns(n, slot, out):
                e.wait_ge(lo_ready, n + 1)
                for k in range(KC):
                    last = product(out, (w_hi[slot][:, k, :], w_lo[slot][:, k, :]),
                                   (h_hi[:, k, :], h_lo[:, k, :]), k == 0, k == KC - 1)
                last.then_inc(block_used, 1)

            def rows(n, slot, out):
                e.wait_ge(lo_ready, n + 1)
                for b in range(TH):
                    cols = slice(P * b, P * b + P)
                    for k in range(KC):
                        last = product(out[:, cols], (h_hi[:, k, cols], h_lo[:, k, cols]),
                                       (w_hi[slot][:, k, :], w_lo[slot][:, k, :]), k == 0, k == KC - 1)
                last.then_inc(block_used, 1)

            def mean_squares(i):
                e.wait_ge(squares, i + 1)
                for k in range(KC):
                    last = e.matmul(ps[:, 7, 0:T], mean_w, norm_a[:, k, :], start=(k == 0), stop=(k == KC - 1))
                last.then_inc(mean_ready, 1)

            def index_scores(b):
                S = P * (b + 1)
                if b == 0:
                    e.wait_ge(evac_v, evac[2][1])
                else:
                    e.wait_ge(relu_ready, 4 * b)
                for h in range(8):
                    g, a = h % 4, h // 4
                    rowg = slice(32 * g, 32 * g + 32)
                    for z in range(2):
                        last = e.matmul(ps[:, 4 + g, 256 * a:256 * a + S], qi[rowg, a, z, P * b:P * b + P],
                                        ki[rowg, z, 0:S], start=(z == 0), stop=(z == 1))
                last.then_inc(isc_ready, 1)

            e.wait_ge(kept_loaded, 16)
            mean_squares(0)
            e.wait_ge(h_ready, 1)
            for n in range(N_IN):
                q = pair_of[n]
                if half_of[n] == 0 and q >= 4:
                    e.wait_ge(*evac[q - 4])
                out = proj_bank(q)[:, 256 * half_of[n]:256 * half_of[n] + 256]
                (rows if PAIRS[q][1] == ROWS else columns)(n, n % RING, out)
                if n == 15:
                    index_scores(0)
                if n == 18:
                    index_scores(1)

            e.wait_ge(evac_v, n_evac_v)
            e.wait_ge(evac_s, n_evac_s)
            e.wait_ge(relu_ready, 8)
            for r in range(RET_H):
                tile, rg = r // 2, slice(64 * (r % 2), 64 * (r % 2) + 64)
                for first, width, jc in ((0, 256, 0), (256, 128, 1)):
                    for z in range(2):
                        last = e.matmul(ps[:, 4 + r, first:first + width], kr[rg, tile, z, P * jc:P * jc + P],
                                        qr[rg, tile, z, P * jc:T], start=(z == 0), stop=(z == 1))
            last.then_inc(inner_ready, 1)
            e.wait_ge(inner_used, 1)
            for r in range(RET_H):
                out = ps[:, r // 2, 256 * (r % 2):256 * (r % 2) + 256]
                e.matmul(out, vr[:, 0, P * r:P * r + P], inner[:, r, 0:256], start=True, stop=False,
                         skip_group_check=True)
                last = e.matmul(out[:, P:T], vr[:, 1, P * r:P * r + P], inner[:, r, 256:384], start=False,
                                stop=True, skip_group_check=True)
            last.then_inc(ret_ready, 1)

            def logits(b):
                S = P * (b + 1)
                if b:
                    e.wait_ge(mix_ready, b + 1)
                for h in range(8):
                    g, a = h % 4, h // 4
                    rowg = slice(32 * g, 32 * g + 32)
                    for z in range(2):
                        last = e.matmul(ps[:, 4 + g, 256 * a:256 * a + S], qa[rowg, a, z, P * b:P * b + P],
                                        ka[rowg, a, z, 0:S], start=(z == 0), stop=(z == 1))
                last.then_inc(logit_ready, 1)

            def group_mean(src, done):
                flat = src.rearrange("p h t -> p (h t)")
                for c in range(2):
                    last = e.matmul(ps[:, 2 + c, :], mean_w, flat[:, 512 * c:512 * c + 512], start=True, stop=True)
                last.then_inc(done, 1)

            logits(0)
            e.wait_ge(ret_copied, 1)
            group_mean(ro, gmean_ready)
            e.wait_ge(centred, 1)
            group_mean(rsq, gvar_ready)
            e.wait_ge(gvar_eps, 1)
            for b in range(TH):
                if b:
                    logits(b)
                e.wait_ge(prob_ready, b + 1)
                for ck in range(b + 1):
                    for k in range(8):
                        last = e.transpose(ps[:, 2 * ck + k // 4, P * (k % 4):P * (k % 4) + P],
                                           prob[:, k, P * ck:P * ck + P], ident)
                last.then_inc(probT_ready, 1)
                e.wait_ge(probT_copied, (b + 1) * (b + 2) // 2)
                for h in range(8):
                    k = 2 * (h % 4) + h // 4
                    out = ps[64 * (h % 2):64 * (h % 2) + 64, 4, P * (h // 2):P * (h // 2) + P]
                    for ck in range(b + 1):
                        last = e.matmul(out, va[:, ck, 64 * h:64 * h + 64], probT[:, ck, k, :],
                                        start=(ck == 0), stop=(ck == b))
                last.then_inc(att_ready, 1)

            e.wait_ge(mix_ready, 1 + TH)
            for c in range(N_OUT):
                if c >= 4:
                    e.wait_ge(out_added, c - 3)
                n = FIRST_OUT + c
                columns(n, n % RING, ps[:, c % 4, 0:T])
            mean_squares(1)
            e.wait_ge(h_ready, 2)
            for c in range(N_PQ):
                if c >= 4:
                    e.wait_ge(qry_copied, c - 3)
                n = FIRST_PQ + c
                columns(n, n % RING, ps[:, c % 4, 0:T])
            e.wait_ge(qry_copied, N_PQ)
            e.wait_ge(sk_loaded, 16)
            for b in range(TH):
                if b:
                    e.wait_ge(score_copied, b)
                for c in range(N_PQ):
                    last = e.matmul(ps[:, 4 + c // 4, P * (c % 4):P * (c % 4) + P], qry[:, c, P * b:P * b + P],
                                    sk[:, c, :], start=True, stop=True)
                last.then_inc(score_ready, 1)

            for j in range(RING):
                columns(FIRST_U + j, (FIRST_U + j) % RING, ps[:, j, 0:T])
            with e.Fori(1, NKEYS // RING) as i:
                for j in range(RING):
                    e.wait_ge(gelu_ready, i * RING + (j - RING + 1))
                    columns(i * RING + (FIRST_U + j), (FIRST_U + j) % RING, ps[:, j, 0:T])

            e.wait_ge(sel_rows, 1)
            for w in range(3):
                for b in range(TH):
                    last = e.transpose(ps[:, 4 + w // 2, (w % 2) * T + P * b:(w % 2) * T + P * b + P],
                                       sel[:, w, P * b:P * b + P], ident)
            last.then_inc(sel_T, 1)

            def gate_row(t, j, bank):
                e.wait_ge(hot_ready, t + 1)
                e.matmul(ps[:, bank, P * (j % 4):P * (j % 4) + P], hot_l[j % 2][:], hot_r[j % 2][:],
                         start=True, stop=True).then_inc(hot_used, 1)

            for j in range(8):
                gate_row(j, j, 4 + j // 4)
            with e.Fori(1, T // 8) as i:
                for j in range(8):
                    if j % 4 == 0:
                        e.wait_ge(gates_used, i * 2 + (j // 4 - 1))
                    gate_row(i * 8 + j, j, 4 + j // 4)
            e.wait_ge(gates_used, T // 4)

            def mix_experts(i2, j, start, stop):
                slot = (FIRST_V + j) % RING
                e.wait_ge(wexp_lo, i2 + 1)
                e.wait_ge(lo_ready, i2 + (FIRST_V + 1))
                for c in range(KC):
                    last = product(ps[:, 4 + c // 2, (c % 2) * T:(c % 2) * T + T],
                                   (w_hi[slot][:, c, :], w_lo[slot][:, c, :]),
                                   (h_hi[:, j, :], h_lo[:, j, :]), start and c % 2 == 0, stop, check=False)
                last.then_inc(block_used, 1)

            for j in range(RING):
                mix_experts(j, j, j == 0, False)
            with e.Fori(1, NKEYS // RING - 1) as i:
                for j in range(RING):
                    mix_experts(i * RING + j, j, False, False)
            for j in range(RING):
                mix_experts(NKEYS - RING + j, j, False, j == RING - 1)
            mean_squares(2)


def _rope_tables():
    t = np.arange(T, dtype=np.float32)

    def cs(inv, copies):
        ang = t[None, :] * inv[:, None]
        c = np.tile(np.cos(ang), (copies, 1)).astype(np.float32)
        s = np.tile(np.sin(ang), (copies, 1)).astype(np.float32)
        return [c, s, s, c]

    att = (1.0 / (np.float32(10000.0) ** (np.arange(0, ATT_D, 2, dtype=np.float32) / ATT_D))).astype(np.float32)
    ret = (1.0 / (np.float32(10000.0) ** np.linspace(0.0, 1.0, RET_D // 2, dtype=np.float32))).astype(np.float32)
    log_g = np.log(1.0 - 2.0 ** (-5.0 - np.arange(RET_H, dtype=np.float64)))
    diff = np.arange(T)[None, :] - np.arange(P)[:, None]
    decay = [np.where(diff >= 0, np.exp(g * np.maximum(diff, 0)), 0.0) * RET_D ** -0.5 for g in log_g]
    causal = np.where(np.arange(P)[None, :] <= np.arange(P)[:, None], 0.0, NEG)
    tab = np.concatenate(cs(att, 4) + cs(ret, 2) + decay + [causal], axis=1).astype(np.float32)
    keep = np.stack([np.tile(np.arange(P), (P, 1)), np.eye(P), np.full((P, P), 1.0 / P)], axis=1).astype(np.float32)
    return np.ascontiguousarray(tab), np.ascontiguousarray(keep)


def _blocks(w):
    n = w.shape[1] // P
    return w.reshape(KC, P, n, P).transpose(2, 1, 0, 3).reshape(n, P, KC * P)


def _in_columns():
    at = dict(qa=0, ka=512, va=1024, qi=1536, ki=2048, wi=2112, qr=2120, kr=2632, vr=3144, gr=3656)
    out = []
    for name, kind, _ in PAIRS:
        base, i = at[name[:2]], int(name[2:] or 0)
        if name == "wi":
            out += [base + c for c in range(ATT_H)] + [-1] * (P - ATT_H)
        elif kind != ROT:
            out += range(base + 256 * i, base + 256 * i + 256)
        else:
            heads, half = (2, 64) if name[1] == "r" else (4, 32)
            for z in range(2):
                for g in range(heads):
                    head = 0 if name == "ki" else heads * i + g
                    out += [base + head * 2 * half + z * half + j for j in range(half)]
    return np.array(out)


def kernel(x, c, w_ada, b_ada, norm_mix_g, w_in, w_out, norm_ffn_g, w_pq, sub_keys, u_emb, v_emb, norm_final_g):
    import concourse.bacc as bacc
    from concourse.bass_utils import run_bass_kernel_spmd as run

    x, c, w_ada, b_ada, norm_mix_g, w_in, w_out, norm_ffn_g, w_pq, sub_keys, u_emb, v_emb, norm_final_g = (
        np.asarray(a) for a in (x, c, w_ada, b_ada, norm_mix_g, w_in, w_out, norm_ffn_g, w_pq, sub_keys,
                                u_emb, v_emb, norm_final_g))

    def columns(v):
        return v.reshape(-1, P).T

    tab, keep = _rope_tables()
    cols = _in_columns()
    w_cols = np.concatenate([w_in[0], np.zeros((D, 1), np.float32)], axis=1)[:, cols]
    arrays = {
        "xT": x[0].reshape(T, KC, P).transpose(2, 1, 0),
        "c_rows": np.broadcast_to(c[0], (P, D)),
        "w_ada": w_ada[0].T.reshape(ADA_LOADS, ADA_GROUP, P, D).transpose(0, 2, 1, 3).reshape(ADA_LOADS, P, -1),
        "b_ada": columns(b_ada[0]),
        "gains": np.stack([columns(norm_mix_g[0]), columns(norm_ffn_g[0]), columns(norm_final_g)], axis=1),
        "tables": tab,
        "keep": keep,
        "early": np.concatenate([_blocks(w_cols), _blocks(w_out[0]), _blocks(w_pq[0])]),
        "skeys": sub_keys[0].reshape(2 * PEER_H, NKEYS, P).transpose(2, 0, 1),
        "u": u_emb[0].reshape(NKEYS, NKEYS, KC, P).transpose(1, 3, 2, 0).reshape(NKEYS, P, KC * P),
        "v": v_emb[0].reshape(NKEYS, NKEYS, D).transpose(1, 0, 2),
    }
    nc = bacc.Bacc("TRN2", target_bir_lowering=False, num_devices=1)
    sent, args = {}, []
    for name, a in arrays.items():
        sent[name] = np.ascontiguousarray(a)
        args.append(nc.dram_tensor(name, a.shape, F32, kind="ExternalInput").ap())
    args.append(nc.dram_tensor("outT", (P, KC, T), F32, kind="ExternalOutput").ap())
    build(nc, *args)
    r = run(nc, [sent], core_ids=[0])
    y = np.asarray(r.results[0]["outT"])
    return np.ascontiguousarray(y.transpose(2, 1, 0).reshape(1, T, D))
```

```python
from contextlib import ExitStack

import numpy as np

import concourse.bass as bass
from concourse import mybir

F32 = mybir.dt.float32
F32R = mybir.dt.float32r
U32 = mybir.dt.uint32
ALU = mybir.AluOpType
ACT = mybir.ActivationFunctionType
AX_X = mybir.AxisListType.X

P = 128
D = 1024
KC = D // P
T = 256
TH = T // P
ATT_H, ATT_D = 8, 64
RET_H, RET_D = 4, 128
TOPK = min(256, T // 4)
PEER_H, NKEYS, PTOP = 8, 128, 16
EPS = 1e-6
N_MOD = 6
N_PICKS = TH * PEER_H
PICK_TURNS = 4
PICKS = N_PICKS // PICK_TURNS
PICK_BLOCKS = 12
DECODE_BLOCKS = 8
PICK_LINKS = 11
DECODE_LINKS = 9
HK = PEER_H * PTOP
KEYS_H = NKEYS // 2
GROUP = 4
GROUPS = T // GROUP

ROT = "rotate"
ROWS = "rows"
GATE = "gate"
PAIRS = [("ki", ROT, 2), ("qi0", ROT, 2), ("qi1", ROT, 2), ("wi", ROWS, 1),
         ("ka0", ROT, 2), ("va0", ROWS, 2), ("ka1", ROT, 2), ("va1", ROWS, 2), ("qa0", ROT, 2), ("qa1", ROT, 2),
         ("kr0", ROT, 2), ("kr1", ROT, 2), ("qr0", ROT, 2), ("vr0", ROWS, 2), ("qr1", ROT, 2), ("vr1", ROWS, 2),
         ("gr0", GATE, 2), ("gr1", GATE, 2)]
PROJ_BANKS = 3
INDEX_AFTER = (8, 11)
LOGITS_AFTER = (19, 24)
PROBT_AFTER = (23, 28)
ATT_AFTER = (24, 30)
INNER_AFTER = 30
RET_AFTER = 32
INDEX_AT = (12, 15)
PICK_AT = ((13, 14, 16), tuple(range(17, 23)))
SOFTMAX_AT = (23, 28)
PROBT_AT = (27, 32)
ATT_AT = (28, 34)
INNER_AT = 34
RET_AT = 36
ADA_AT = [n for n in range(6, 39) if n not in (12, 15, 23, 24, 28, 29, 34, 37, 38)]
N_IN = sum(p[2] for p in PAIRS)
N_OUT = KC
N_PQ = 2 * PEER_H
FIRST_OUT = N_IN
FIRST_PQ = FIRST_OUT + N_OUT
N_EARLY = FIRST_PQ + N_PQ
FIRST_U = N_EARLY
FIRST_V = FIRST_U + NKEYS
RING = 4
ADA_GROUP = 4
N_ADA = N_MOD * KC
ADA_LOADS = N_ADA // ADA_GROUP
ADA_SLOTS = 2
NEG = -1.0e30
TAKEN = -3.0e38

TAB = dict(att_cs=(0, 512), att_sc=(512, 1024), ret_cs=(1024, 1536), ret_sc=(1536, 2048),
           decay=(2048, 3072), causal=(3072, 3200))
TAB_W = 3200


def build(nc, xT, cb, ada, ada_b, gains, tables, keep, early, skeys, uw, vw, outT):
    with ExitStack() as ctx:
        def sb(name, shape, dt=F32):
            return ctx.enter_context(nc.sbuf_tensor(name, shape, dt))

        def sem(name):
            return ctx.enter_context(nc.semaphore(name))

        act = sb("act", [P, NKEYS * T])
        h_hi = sb("h_hi", [P, KC, T], F32R)
        h_lo = sb("h_lo", [P, KC, T], F32R)
        x = sb("x", [P, KC, T])
        raw = [sb(f"raw{s}", [P, KC * P]) for s in range(RING)]
        all_hi = sb("w_hi", [P, RING, KC, P], F32R)
        all_lo = sb("w_lo", [P, RING, KC, P], F32R)
        w_hi = [all_hi[:, s] for s in range(RING)]
        w_lo = [all_lo[:, s] for s in range(RING)]
        kept = sb("kept", [P, 3, P])
        iota, ident, mean_w = kept[:, 0, :], kept[:, 1, :], kept[:, 2, :]
        sel = sb("sel", [P, 3, T])
        mod = sb("mod", [P, N_ADA])
        mod_b = sb("mod_b", [P, N_ADA])
        gain = sb("gain", [P, 3, KC])
        gmod = sb("gmod", [P, 2, KC])
        gsum = sb("gsum", [P, TH * PEER_H])

        x_flat = x[:].rearrange("p k t -> p (k t)")
        hot_l = [x_flat[:, GROUP * P * s:GROUP * P * (s + 1)].rearrange("p (t i) -> p t i", t=GROUP)
                 for s in range(2)]
        hot_k = [x_flat[:, 1024 + GROUP * KEYS_H * s:1024 + GROUP * KEYS_H * (s + 1)].rearrange(
            "p (t i) -> p t i", t=GROUP) for s in range(2)]
        hot_r = [x_flat[:, 1536 + GROUP * KEYS_H * s:1536 + GROUP * KEYS_H * (s + 1)].rearrange(
            "p (t i) -> p t i", t=GROUP) for s in range(2)]

        top = [0]

        def scratch(*dims, at=None):
            n = int(np.prod(dims))
            if at is None:
                at = top[0]
                top[0] += n
            assert at + n <= NKEYS * T, (at, n)
            v = act[:, at:at + n]
            if len(dims) == 2:
                v = v.rearrange("p (a b) -> p a b", a=dims[0])
            elif len(dims) == 3:
                v = v.rearrange("p (a b c) -> p a b c", a=dims[0], b=dims[1])
            return v

        ada_ring = scratch(ADA_SLOTS, ADA_GROUP, D)
        c_row = scratch(D)
        tab = scratch(TAB_W)
        rot_a = scratch(2, T)
        rot_b = scratch(2, T)
        ka = scratch(2, 2, T)
        qa = scratch(2, 2, T)
        qi = scratch(2, 2, T)
        ki = scratch(2, T)
        kr = scratch(2, 2, T)
        qr = scratch(2, 2, T)
        gr = scratch(4, T)
        va = scratch(TH, 512)
        vr = scratch(TH, 512)
        wi = scratch(TH, 8)
        att_o = scratch(4, T)
        isc = scratch(TH, T)
        best = scratch(8)
        mask = scratch(TH, T)
        inner = scratch(RET_H, 384)
        rmax = scratch(8)
        rsum = scratch(8)
        rinv = scratch(8)
        c_tmp = va.rearrange("p a b -> p (a b)")
        shared = top[0]
        norm_fin = scratch(KC, T, at=0)
        norm_a = scratch(KC, T, at=shared)
        norm_b = scratch(KC, T, at=shared + 2048)
        relu = scratch(8, T, at=shared)
        prob = scratch(8, T, at=shared)
        probT = scratch(2, 8, P, at=shared + 2048)
        rstd = scratch(T, at=shared + 4096)
        ro = scratch(4, T, at=shared + 4096 + 256)
        rsq = scratch(4, T, at=shared + 5120 + 256)
        assert shared + 6400 <= NKEYS * T
        top[0] = NKEYS * T // 2
        qry = scratch(2 * PEER_H, T)
        sk = scratch(2 * PEER_H, NKEYS)
        score = scratch(TH, PEER_H, 2 * NKEYS)
        wk = [scratch(2, NKEYS) for _ in range(2)]
        val = scratch(2, PTOP)
        idx = scratch(2, PTOP)
        cand = scratch(PTOP, PTOP)
        cval = scratch(PTOP)
        cpos = scratch(PTOP)
        top_p = scratch(TH, HK)
        key1 = scratch(TH, HK)
        key2 = scratch(TH, HK)
        rank_u = scratch(HK)
        rank_f = scratch(2, HK)
        hit = scratch(HK, PTOP)
        assert top[0] <= NKEYS * T, top[0]

        def u32(ap):
            return ap.bitcast(U32)

        def tb(name):
            return tab[:, TAB[name][0]:TAB[name][1]]

        ps = ctx.enter_context(nc.psum_tensor("ps", [P, 8, 512], F32))

        x_loaded = sem("x_loaded")
        c_loaded = sem("c_loaded")
        small_loaded = sem("small_loaded")
        tab_loaded = sem("tab_loaded")
        kept_loaded = sem("kept_loaded")
        sk_loaded = sem("sk_loaded")
        ada_loaded = [sem(f"ada_loaded{s}") for s in range(ADA_SLOTS)]
        raw_loaded = [sem(f"raw_loaded{s}") for s in range(RING)]
        hi_ready = sem("hi_ready")
        lo_ready = sem("lo_ready")
        block_used = sem("block_used")
        c_exp = sem("c_exp")
        ada_used = sem("ada_used")
        squares = sem("squares")
        mean_ready = sem("mean_ready")
        mean_eps = sem("mean_eps")
        root_ready = sem("root_ready")
        normed = sem("normed")
        h_hi_ready = sem("h_hi_ready")
        h_ready = sem("h_ready")
        chain = sem("chain")
        evac_v = sem("evac_v")
        evac_s = sem("evac_s")
        gate_exp = sem("gate_exp")
        isc_ready = sem("isc_ready")
        relu_ready = sem("relu_ready")
        relu_used = sem("relu_used")
        logit_ready = sem("logit_ready")
        logit_used = sem("logit_used")
        shifted = sem("shifted")
        exp_ready = sem("exp_ready")
        prob_ready = sem("prob_ready")
        probT_ready = sem("probT_ready")
        probT_copied = sem("probT_copied")
        att_ready = sem("att_ready")
        att_copied = sem("att_copied")
        mix_hi = sem("mix_hi")
        inner_ready = sem("inner_ready")
        inner_used = sem("inner_used")
        ret_ready = sem("ret_ready")
        ret_copied = sem("ret_copied")
        gmean_ready = sem("gmean_ready")
        centred = sem("centred")
        gvar_ready = sem("gvar_ready")
        gvar_eps = sem("gvar_eps")
        groot = sem("groot")
        ret_done = sem("ret_done")
        ret_hi = sem("ret_hi")
        mix_ready = sem("mix_ready")
        out_added = sem("out_added")
        qry_copied = sem("qry_copied")
        score_ready = sem("score_ready")
        score_copied = sem("score_copied")
        gelu_ready = sem("gelu_ready")
        searches = sem("searches")
        picked = sem("picked")
        decoded = sem("decoded")
        pick_exp = sem("pick_exp")
        sel_rows = sem("sel_rows")
        sel_T = sem("sel_T")
        sel_ready = sem("sel_ready")
        score_taken = sem("score_taken")
        score_free = sem("score_free")
        x_stored = sem("x_stored")
        hot_ready = sem("hot_ready")
        gated = sem("gated")
        hot_used = sem("hot_used")
        gates_used = sem("gates_used")
        wexp_hi = sem("wexp_hi")
        wexp_lo = sem("wexp_lo")
        out_ready = sem("out_ready")
        stored = sem("stored")

        block = ctx.enter_context(nc.Block())

        evac = []
        nv = ns = 0
        for _, kind, _ in PAIRS:
            if kind == ROWS:
                ns += 1
                evac.append((evac_s, ns))
            else:
                nv += 1
                evac.append((evac_v, nv))
        n_evac_v, n_evac_s = nv, ns
        pair_of, half_of, last_of = [], [], []
        for q, (_, _, blocks) in enumerate(PAIRS):
            for i in range(blocks):
                pair_of.append(q)
                half_of.append(i)
            last_of.append(len(pair_of) - 1)

        def mean_bank(i):
            return 0 if i == 2 else 7

        def proj_bank(q):
            return ps[:, q % PROJ_BANKS, :]

        @block.sync
        def _(sp):
            sp.dma_start(x[:], xT).then_inc(x_loaded, 16)
            sp.dma_start(kept[:], keep).then_inc(kept_loaded, 16)

            def load(source, slot):
                sp.dma_start(raw[slot][:], source).then_inc(raw_loaded[slot], 16)

            sp.wait_ge(ada_loaded[0], 16)
            for n in range(RING):
                load(early[n], n)
            sp.dma_start(tab, tables).then_inc(tab_loaded, 16)
            rounds = N_EARLY // RING
            with sp.Fori(1, rounds) as i:
                for s in range(RING):
                    sp.wait_ge(lo_ready, i * RING + s - RING + 1)
                    sp.dma_start(raw[s][:], early[bass.ds(i * RING + s, 1)].rearrange("a p n -> (a p) n")
                                 ).then_inc(raw_loaded[s], 16)
            for n in range(rounds * RING, N_EARLY):
                sp.wait_ge(lo_ready, n - RING + 1)
                load(early[n], n % RING)
            sp.wait_ge(out_added, KC)
            sp.dma_start(sk, skeys).then_inc(sk_loaded, 16)
            sp.dma_start(outT, x[:]).then_inc(x_stored, 16)
            for first, source in ((FIRST_U, uw), (FIRST_V, vw)):
                with sp.Fori(0, NKEYS // RING) as i:
                    for j in range(RING):
                        s = (first + j) % RING
                        sp.wait_ge(lo_ready, i * RING + (first + j - RING + 1))
                        sp.dma_start(raw[s][:], source[bass.ds(i * RING + j, 1)].rearrange("a p n -> (a p) n")
                                     ).then_inc(raw_loaded[s], 16)
            sp.wait_ge(gates_used, 2 * GROUPS)
            sp.wait_ge(x_stored, 16)
            sp.dma_start(x[:], outT).then_inc(x_loaded, 16)
            for c in range(4):
                sp.wait_ge(out_ready, c + 1)
                sp.dma_start(outT[:, c * KC // 4:(c + 1) * KC // 4, :],
                             norm_fin[:, c * KC // 4:(c + 1) * KC // 4, :]).then_inc(stored, 16)
            sp.wait_ge(stored, 64)

        @block.gpsimd
        def _(pool):
            pool.dma_start(c_row, cb).then_inc(c_loaded, 16)
            pool.dma_start(mod_b[:], ada_b).then_inc(small_loaded, 16)
            pool.dma_start(gain[:], gains).then_inc(small_loaded, 16)
            for n in range(ADA_LOADS):
                if n >= ADA_SLOTS:
                    pool.wait_ge(ada_used, (n - ADA_SLOTS + 1) * ADA_GROUP)
                pool.dma_start(ada_ring[:, n % ADA_SLOTS].rearrange("p g k -> p (g k)"), ada[n]).then_inc(ada_loaded[n % ADA_SLOTS], 16)

        @block.scalar
        def _(e):
            def split_hi(n, slot, turn):
                e.wait_ge(raw_loaded[slot], turn * 16)
                if not isinstance(n, int) or n >= RING:
                    e.wait_ge(block_used, n - RING + 1)
                e.activation(w_hi[slot], raw[slot][:].rearrange("p (k m) -> p k m", k=KC),
                             ACT.Copy).then_inc(hi_ready, 1)

            def square(i, k):
                if i:
                    e.wait_ge(out_added, (i - 1) * KC + k + 1)
                e.activation(norm_a[:, k, :], x[:, k, :], ACT.Square).then_inc(squares, 1)

            def root(i):
                e.wait_ge(mean_eps, i + 1)
                e.activation(rstd, rstd, ACT.Sqrt).then_inc(root_ready, 1)

            def norm_hi(i):
                at = 0 if i == 0 else 3 * KC
                for k in range(KC):
                    e.wait_ge(normed, i * KC + k + 1)
                    e.activation(h_hi[:, k, :], norm_b[:, k, :], ACT.Identity,
                                 bias=mod[:, at + k:at + k + 1]).then_inc(h_hi_ready, 1)

            e.wait_ge(c_loaded, 16)
            e.activation(c_tmp, c_row, ACT.Exp, scale=-1.0).then_inc(c_exp, 1)
            e.wait_ge(x_loaded, 16)
            for k in range(KC):
                square(0, k)
            root(0)
            for n in range(RING):
                split_hi(n, n, 1)
            norm_hi(0)

            def take(q):
                name, kind, _ = PAIRS[q]
                e.wait_ge(block_used, last_of[q] + 1)
                src = proj_bank(q)
                if kind == GATE:
                    i = int(name[-1])
                    e.activation(gr[:, 2 * i:2 * i + 2, :], src.rearrange("p (a b) -> p a b", a=2), ACT.Exp,
                                 scale=-1.0).then_inc(gate_exp, 1)
                elif name == "wi":
                    e.activation(wi, src.rearrange("p (a b) -> p a b", a=TH)[:, :, 0:8], ACT.Copy,
                                 scale=float(ATT_H) ** -0.5).then_inc(evac_s, 1)
                else:
                    i = int(name[-1])
                    dst = (va if name[1] == "a" else vr)[:, :, 256 * i:256 * i + 256]
                    e.activation(dst, src.rearrange("p (t c) -> p t c", t=TH), ACT.Copy).then_inc(evac_s, 1)

            def index_relu(b):
                S = P * (b + 1)
                e.wait_ge(isc_ready, b + 1)
                if b:
                    e.wait_ge(relu_used, b)
                for g in range(4):
                    e.activation(relu[:, 2 * g:2 * g + 2, 0:S],
                                 ps[:, 4 + g, :].rearrange("p (a s) -> p a s", a=2)[:, :, 0:S], ACT.Relu,
                                 scale=0.125).then_inc(relu_ready, 1)

            def softmax_exp(b):
                e.wait_ge(shifted, b + 1)
                for h in range(8):
                    e.activation(prob[:, h, 0:P * (b + 1)], prob[:, h, 0:P * (b + 1)], ACT.Exp, bias=rmax[:, h:h + 1],
                                 accum_out=rsum[:, h:h + 1]).then_inc(exp_ready, 1)

            def take_probT(b):
                e.wait_ge(probT_ready, b + 1)
                for ck in range(b + 1):
                    e.activation(probT[:, ck].rearrange("p (a h) t -> p a h t", a=2),
                                 ps[:, 4 + 2 * ck:6 + 2 * ck, :].rearrange("p a (h t) -> p a h t", h=4), ACT.Copy
                                 ).then_inc(probT_copied, 1)

            def take_att(b):
                e.wait_ge(att_ready, b + 1)
                e.activation(att_o[:, :, P * b:P * b + P], ps[:, 3, :].rearrange("p (a t) -> p a t", a=4),
                             ACT.Copy).then_inc(att_copied, 1)

            for n in range(RING, N_IN + RING):
                split_hi(n, n % RING, n // RING + 1)
                if n - 3 < N_IN and n - 3 == last_of[pair_of[n - 3]] and PAIRS[pair_of[n - 3]][1] != ROT:
                    take(pair_of[n - 3])
                for b in range(TH):
                    if n == INDEX_AT[b]:
                        index_relu(b)
                    if n == PROBT_AT[b]:
                        take_probT(b)
                    if n == ATT_AT[b]:
                        take_att(b)
                    if n == SOFTMAX_AT[b]:
                        softmax_exp(b)
                if n == RET_AT:
                    e.wait_ge(ret_ready, 1)
                    e.activation(ro, ps[:, 4:6, :].rearrange("p a (b t) -> p (a b) t", b=2),
                                 ACT.Copy).then_inc(ret_copied, 1)
            e.wait_ge(block_used, N_IN)
            e.wait_ge(att_copied, TH)
            e.activation(h_hi[:, 0:4, :], att_o, ACT.Copy).then_inc(mix_hi, 1)
            e.wait_ge(gvar_eps, 1)
            e.activation(rsq, rsq, ACT.Sqrt).then_inc(groot, 1)
            e.wait_ge(ret_done, 1)
            e.activation(h_hi[:, 4:8, :], ro, ACT.Copy).then_inc(ret_hi, 1)
            for c in range(KC):
                n = FIRST_OUT + RING + c
                if c < RING:
                    split_hi(n, n % RING, n // RING + 1)
                square(1, c)
                if c >= RING:
                    split_hi(n, n % RING, n // RING + 1)
            root(1)
            norm_hi(1)

            def take_query(i):
                e.wait_ge(block_used, FIRST_PQ + i + 1)
                e.activation(qry[:, i, :], ps[:, i % 4, 0:T], ACT.Copy).then_inc(qry_copied, 1)

            for n in range(FIRST_PQ + RING, N_EARLY + RING):
                split_hi(n, n % RING, n // RING + 1)
                take_query(n - FIRST_PQ - RING)
            for b in range(TH):
                e.wait_ge(score_ready, b + 1)
                e.activation(score[:, b].rearrange("p (a h) n -> p a (h n)", a=4), ps[:, 4:8, :],
                             ACT.Copy).then_inc(score_copied, 1)
            e.wait_ge(ada_used, N_ADA)
            e.preload_act_table(ACT.Gelu)

            def gelu(n, i2, bank):
                e.wait_ge(block_used, n + 1)
                e.activation(act[:, bass.ds(i2 * T, T)], ps[:, bank, 0:T], ACT.Gelu).then_inc(gelu_ready, 1)

            def expert_round(i, blocks, first, before=lambda j: None, after=lambda j: None):
                for j in range(blocks):
                    n = FIRST_U + first + RING + j
                    before(j)
                    split_hi(i * blocks + n, n % RING, i * (blocks // RING) + (n // RING + 1))
                    gelu(i * blocks + (n - RING), i * blocks + (first + j), (first + j) % RING)
                    after(j)

            def gate_rows(half, g, s):
                e.wait_ge(hot_ready, g + (half * GROUPS + 1))
                for t in range(GROUP):
                    last = e.activation(hot_r[s][:, t, :], hot_k[s][:, t, :], ACT.Copy,
                                        scale=sel[:, 2, :][:, bass.ds(g * GROUP + t, 1)])
                last.then_inc(gated, 1)

            with e.Fori(0, PICK_TURNS) as i:
                def before(j):
                    if j % 3 == 0:
                        c = j // 3
                        e.wait_ge(score_free, i * PICKS + (c + 1))
                        e.activation(wk[c % 2].rearrange("p a n -> p (a n)"),
                                     score.rearrange("p a h n -> p (a h n)")[:, bass.ds((i * PICKS + c) * (2 * NKEYS),
                                                                                       2 * NKEYS)],
                                     ACT.Copy).then_inc(score_taken, 1)
                expert_round(i, PICK_BLOCKS, 0, before)
            e.wait_ge(picked, N_PICKS)
            e.activation(sel[:, 2, :], sel[:, 2, :], ACT.Exp).then_inc(pick_exp, 1)
            e.preload_act_table(ACT.Gelu)
            first = PICK_TURNS * PICK_BLOCKS
            with e.Fori(0, TH) as i:
                expert_round(i, DECODE_BLOCKS, first)
            e.wait_ge(decoded, TH)
            gate_rows(0, 0, 0)
            rounds = GROUPS // RING
            with e.Fori(0, rounds - 1) as i:
                expert_round(i, RING, NKEYS - GROUPS, after=lambda j: gate_rows(0, i * RING + (j + 1), (j + 1) % 2))
            expert_round(rounds - 1, RING, NKEYS - GROUPS,
                         after=lambda j: gate_rows(0, GROUPS - RING + j + 1, (j + 1) % 2) if j + 1 < RING else
                         gate_rows(1, 0, 0))

            def expert_hi(i2, slot):
                e.activation(h_hi[:, slot, :], act[:, bass.ds(i2 * T, T)], ACT.Copy).then_inc(wexp_hi, 1)

            e.wait_ge(gates_used, GROUPS)
            for j in range(RING):
                expert_hi(j, j)
            for g in range(1, RING + 1):
                gate_rows(1, g, g % 2)

            def mix_round(i, last=False):
                for j in range(RING):
                    n = FIRST_V + RING + j
                    split_hi(i * RING + n, n % RING, i + (n // RING + 1))
                    expert_hi(i * RING + (RING + j), j)
                    if not (last and j + 1 == RING):
                        gate_rows(1, i * RING + (RING + j + 1), (j + 1) % 2)

            n_first = (NKEYS - GROUPS) // RING - 1
            with e.Fori(0, n_first - 1) as i:
                mix_round(i)
            mix_round(n_first - 1, last=True)
            e.wait_ge(gates_used, 2 * GROUPS)
            with e.Fori(n_first, NKEYS // RING - 1) as i:
                for j in range(RING):
                    n = FIRST_V + RING + j
                    split_hi(i * RING + n, n % RING, i + (n // RING + 1))
                    expert_hi(i * RING + (RING + j), j)
            for k in range(KC):
                square(2, k)
            root(2)

        @block.vector
        def _(e):
            base, steps = [0], [0]

            def link(ins, search=False):
                steps[0] += 1
                ins.then_inc(chain, 1)
                e.wait_ge(chain, base[0] + steps[0])
                if search:
                    e.sem_inc(searches, 1)

            def split_lo(n, slot):
                e.wait_ge(hi_ready, n + 1)
                e.tensor_tensor(w_lo[slot], raw[slot][:].rearrange("p (k m) -> p k m", k=KC),
                                w_hi[slot].bitcast(F32), ALU.subtract).then_inc(lo_ready, 1)

            def ada_block(m):
                load = m // ADA_GROUP
                e.wait_ge(ada_loaded[load % ADA_SLOTS], 16 * (load // ADA_SLOTS + 1))
                w = ada_ring[:, load % ADA_SLOTS, m % ADA_GROUP, :]
                e.tensor_tensor_reduce(w, w, c_row, 1.0, 0.0, ALU.mult, ALU.add,
                                       mod[:, m:m + 1]).then_inc(ada_used, 1)
                if m % ADA_GROUP == ADA_GROUP - 1:
                    a = m + 1 - ADA_GROUP
                    e.wait_ge(ada_used, m + 1)
                    link(e.tensor_tensor(mod[:, a:m + 1], mod[:, a:m + 1], mod_b[:, a:m + 1], ALU.add))

            def gain_mod(i):
                a = KC if i == 0 else 4 * KC
                link(e.scalar_tensor_tensor(out=gmod[:, i, :], in0=mod[:, a:a + KC], scalar=1.0,
                                            in1=gain[:, i, :], op0=ALU.add, op1=ALU.mult))

            def norm(i):
                e.wait_ge(mean_ready, i + 1)
                e.tensor_scalar(rstd, ps[:, mean_bank(i), 0:T], 1.0 / KC, EPS, ALU.mult, ALU.add).then_inc(mean_eps, 1)

            def norm_end(i):
                e.wait_ge(root_ready, i + 1)
                link(e.reciprocal(rstd, rstd))

            def norm_in(i):
                at = 0 if i == 0 else 3 * KC
                for k in range(KC + 1):
                    if k < KC:
                        e.scalar_tensor_tensor(out=norm_b[:, k, :], in0=x[:, k, :], scalar=gmod[:, i, k:k + 1],
                                               in1=rstd, op0=ALU.mult, op1=ALU.mult).then_inc(normed, 1)
                    if k:
                        e.wait_ge(h_hi_ready, i * KC + k)
                        e.scalar_tensor_tensor(out=h_lo[:, k - 1, :], in0=norm_b[:, k - 1, :],
                                               scalar=mod[:, at + k - 1:at + k], in1=h_hi[:, k - 1, :].bitcast(F32),
                                               op0=ALU.add, op1=ALU.subtract).then_inc(h_ready, 1)

            e.wait_ge(c_exp, 1)
            link(e.tensor_scalar(c_tmp, c_tmp, 1.0, None, ALU.add))
            link(e.reciprocal(c_tmp, c_tmp))
            link(e.tensor_tensor(c_row, c_row, c_tmp, ALU.mult))
            norm(0)
            norm_end(0)
            e.wait_ge(small_loaded, 32)
            for m in range(2 * KC - RING):
                ada_block(m)
            for n in range(RING):
                ada_block(2 * KC - RING + n)
                split_lo(n, n)
            gain_mod(0)
            norm_in(0)

            dest = dict(ki=(ki,), qi=(qi[:, 0], qi[:, 1]), ka=(ka[:, 0], ka[:, 1]), qa=(qa[:, 0], qa[:, 1]),
                        kr=(kr[:, 0], kr[:, 1]), qr=(qr[:, 0], qr[:, 1]))

            def rotate(q):
                name = PAIRS[q][0]
                out = dest[name[:2]][int(name[2:] or 0)]
                kind = "ret" if name[1] == "r" else "att"
                e.wait_ge(block_used, last_of[q] + 1)
                pair = proj_bank(q)
                e.tensor_tensor(rot_a.rearrange("p a b -> p (a b)"), pair, tb(kind + "_cs"), ALU.mult)
                link(e.tensor_tensor(rot_b.rearrange("p a b -> p (a b)"), pair, tb(kind + "_sc"), ALU.mult))
                e.tensor_tensor(out[:, 0, :], rot_a[:, 0, :], rot_a[:, 1, :], ALU.subtract)
                last = e.tensor_tensor(out[:, 1, :], rot_b[:, 0, :], rot_b[:, 1, :], ALU.add)
                last.then_inc(evac_v, 1)
                e.wait_ge(evac_v, evac[q][1])

            def gate(q):
                i = int(PAIRS[q][0][-1])
                g = gr[:, 2 * i:2 * i + 2, :]
                e.wait_ge(gate_exp, i + 1)
                link(e.tensor_scalar(g, g, 1.0, None, ALU.add))
                link(e.reciprocal(g, g))
                e.tensor_tensor(g, proj_bank(q).rearrange("p (a b) -> p a b", a=2), g, ALU.mult).then_inc(evac_v, 1)
                e.wait_ge(evac_v, evac[q][1])

            def index_sum(b):
                S = P * (b + 1)
                if b == 0:
                    e.wait_ge(evac_s, evac[3][1])
                for k in range(8):
                    g, tile = k // 2, k % 2
                    h = 4 * tile + g
                    e.wait_ge(relu_ready, 4 * b + g + 1)
                    if k == 0:
                        link(e.tensor_scalar(isc[:, b, 0:S], relu[:, k, 0:S], wi[:, b, h:h + 1], None, ALU.mult))
                    else:
                        ins = e.scalar_tensor_tensor(out=isc[:, b, 0:S], in0=relu[:, k, 0:S], scalar=wi[:, b, h:h + 1],
                                                     in1=isc[:, b, 0:S], op0=ALU.mult, op1=ALU.add)
                        if k == 7:
                            ins.then_inc(relu_used, 1)
                            e.wait_ge(relu_used, b + 1)
                        else:
                            link(ins)
                diag = isc[:, b, P * b:P * b + P]
                link(e.tensor_tensor(diag, diag, tb("causal"), ALU.add))

            def index_pick(b, a, z):
                S = P * (b + 1)
                s = isc[:, b, 0:S]
                for _ in range(a, z):
                    link(e.max(best, s))
                    link(e.match_replace(s, best, s, TAKEN))

            def index_mask(b):
                S = P * (b + 1)
                link(e.tensor_scalar(mask[:, b, 0:S], isc[:, b, 0:S], 0.5 * TAKEN, NEG, ALU.is_gt, ALU.mult))
                diag = mask[:, b, P * b:P * b + P]
                link(e.tensor_tensor(diag, diag, tb("causal"), ALU.add))

            e.wait_ge(tab_loaded, 16)
            def softmax_in(b):
                S = P * (b + 1)
                e.wait_ge(logit_ready, b + 1)
                m = mask[:, b, 0:S]
                src = ps[:, 4:8, :].rearrange("p g (a s) -> p (g a) s", a=2)[:, :, 0:S]
                e.scalar_tensor_tensor(out=prob[:, :, 0:S], in0=src, scalar=float(ATT_D) ** -0.5,
                                       in1=m[:, None, :].to_broadcast([P, 8, S]), op0=ALU.mult,
                                       op1=ALU.add).then_inc(logit_used, 1)
                e.wait_ge(logit_used, b + 1)
                link(e.tensor_reduce(rmax, prob[:, :, 0:S], AX_X, ALU.max))
                e.tensor_scalar(rmax, rmax, -1.0, None, ALU.mult).then_inc(shifted, 1)

            def softmax_out(b):
                S = P * (b + 1)
                e.wait_ge(exp_ready, 8 * (b + 1))
                link(e.reciprocal(rinv, rsum))
                e.tensor_tensor(prob[:, :, 0:S], prob[:, :, 0:S], rinv[:, :, None].to_broadcast([P, 8, S]),
                                ALU.mult).then_inc(prob_ready, 1)
                e.wait_ge(prob_ready, b + 1)

            ada_next = 2 * KC
            for n in range(RING, N_IN + RING):
                split_lo(n, n % RING)
                if n - 3 < N_IN and n - 3 == last_of[pair_of[n - 3]]:
                    q = pair_of[n - 3]
                    if PAIRS[q][1] == ROT:
                        rotate(q)
                    elif PAIRS[q][1] == GATE:
                        gate(q)
                for b in range(TH):
                    if n == INDEX_AT[b]:
                        index_sum(b)
                    if n in PICK_AT[b]:
                        k, rounds = PICK_AT[b].index(n), TOPK // 8
                        index_pick(b, rounds * k // len(PICK_AT[b]), rounds * (k + 1) // len(PICK_AT[b]))
                        if n == PICK_AT[b][-1]:
                            index_mask(b)
                    if n == SOFTMAX_AT[b]:
                        softmax_in(b)
                    if n == SOFTMAX_AT[b] + 1:
                        softmax_out(b)
                if n == INNER_AT:
                    e.wait_ge(inner_ready, 1)
                    for r in range(RET_H):
                        pr = ps[:, 4 + r, 0:384]
                        dec_r = tb("decay").rearrange("p (r t) -> p r t", r=RET_H)[:, r, :]
                        e.tensor_tensor(inner[:, r, 0:256], pr[:, 0:256], dec_r, ALU.mult)
                        last = e.tensor_tensor(inner[:, r, 256:384], pr[:, 256:384], dec_r[:, 0:P], ALU.mult)
                    last.then_inc(inner_used, 1)
                if n in ADA_AT:
                    ada_block(ada_next)
                    ada_next += 1
            assert ada_next == 5 * KC

            e.wait_ge(ret_copied, 1)
            e.wait_ge(gmean_ready, 1)
            flat = ps[:, 6:8, :].rearrange("p a (b t) -> p (a b) t", b=2)
            link(e.tensor_tensor(ro, ro, flat, ALU.subtract))
            e.tensor_tensor(rsq, ro, ro, ALU.mult).then_inc(centred, 1)
            e.wait_ge(mix_hi, 1)
            e.tensor_tensor(h_lo[:, 0:4, :], att_o, h_hi[:, 0:4, :].bitcast(F32), ALU.subtract).then_inc(mix_ready, 1)
            e.wait_ge(gvar_ready, 1)
            e.tensor_scalar(rsq, flat, EPS, None, ALU.add).then_inc(gvar_eps, 1)
            link(e.tensor_tensor(ro, ro, gr, ALU.mult))
            e.wait_ge(groot, 1)
            link(e.reciprocal(rsq, rsq))
            e.tensor_tensor(ro, ro, rsq, ALU.mult).then_inc(ret_done, 1)
            e.wait_ge(ret_hi, 1)
            e.tensor_tensor(h_lo[:, 4:8, :], ro, h_hi[:, 4:8, :].bitcast(F32), ALU.subtract).then_inc(mix_ready, 1)

            def add_out(c):
                e.wait_ge(block_used, FIRST_OUT + c + 1)
                e.scalar_tensor_tensor(out=x[:, c, :], in0=ps[:, c % 4, 0:T], scalar=mod[:, 2 * KC + c:2 * KC + c + 1],
                                       in1=x[:, c, :], op0=ALU.mult, op1=ALU.add).then_inc(out_added, 1)

            gain_mod(1)
            for c in range(KC):
                n = FIRST_OUT + RING + c
                if c < RING:
                    split_lo(n, n % RING)
                add_out(c)
                if c >= RING:
                    split_lo(n, n % RING)
            norm(1)
            norm_end(1)
            norm_in(1)
            for n in range(FIRST_PQ + RING, N_EARLY + RING):
                split_lo(n, n % RING)
                if ada_next < N_ADA:
                    ada_block(ada_next)
                    ada_next += 1
            e.sem_inc(score_free, 2)
            start = base[0] + steps[0]
            with e.Fori(0, PICK_TURNS) as i:
                for c in range(PICKS):
                    base[0], steps[0] = i * (PICKS * PICK_LINKS) + (start + c * PICK_LINKS), 0
                    w = wk[c % 2]
                    e.wait_ge(score_taken, i * PICKS + (c + 1))
                    e.sem_inc(searches, 1)
                    los = iter(range(3 * c, 3 * c + 3))

                    def next_lo():
                        n = FIRST_U + RING + next(los)
                        split_lo(i * PICK_BLOCKS + n, n % RING)

                    for half in range(2):
                        v = [val[:, p, 8 * half:8 * half + 8] for p in range(2)]
                        ix = [idx[:, p, 8 * half:8 * half + 8] for p in range(2)]
                        e.max(v[0], w[:, 0, :])
                        link(e.max(v[1], w[:, 1, :]), search=True)
                        e.max_index(u32(ix[0]), v[0], w[:, 0, :])
                        link(e.max_index(u32(ix[1]), v[1], w[:, 1, :]), search=(half == 0))
                        if half == 0:
                            e.match_replace(w[:, 0, :], v[0], w[:, 0, :], TAKEN)
                            link(e.match_replace(w[:, 1, :], v[1], w[:, 1, :], TAKEN))
                            next_lo()
                    link(e.tensor_tensor(cand, val[:, 0, :, None].to_broadcast([P, PTOP, PTOP]),
                                         val[:, 1, None, :].to_broadcast([P, PTOP, PTOP]), ALU.add), search=True)
                    cd = cand.rearrange("p a b -> p (a b)")
                    for half in range(2):
                        v, ix = cval[:, 8 * half:8 * half + 8], cpos[:, 8 * half:8 * half + 8]
                        link(e.max(v, cd), search=True)
                        link(e.max_index(u32(ix), v, cd), search=(half == 0))
                        if half == 0:
                            link(e.match_replace(cd, v, cd, TAKEN))
                        next_lo()
                    at = bass.ds((i * PICKS + c) * PTOP, PTOP)
                    e.tensor_scalar(sel[:, 2, :][:, at], cval, cval[:, 0:1], None, ALU.subtract)
                    e.tensor_copy(key1.rearrange("p a n -> p (a n)")[:, at], u32(idx[:, 0, :])).then_inc(score_free, 1)
                    e.tensor_copy(key2.rearrange("p a n -> p (a n)")[:, at], u32(idx[:, 1, :]))
                    e.tensor_copy(u32(top_p.rearrange("p a n -> p (a n)"))[:, at], u32(cpos)).then_inc(picked, 1)
                    e.wait_ge(picked, i * PICKS + (c + 1))
                    assert steps[0] == PICK_LINKS, steps
            base[0], steps[0] = start + N_PICKS * PICK_LINKS, 0

            start = base[0]
            with e.Fori(0, TH) as i:
                base[0], steps[0] = i * DECODE_LINKS + start, 0
                at = bass.ds(i * HK, HK)
                pos = u32(top_p.rearrange("p a n -> p (a n)"))[:, at]
                ranks = rank_f
                for w, (keys, op, arg) in enumerate(((key1, ALU.logical_shift_right, 4), (key2, ALU.bitwise_and, 15))):
                    link(e.tensor_scalar(u32(rank_u), pos, arg, None, op))
                    link(e.tensor_copy(ranks[:, w, :], u32(rank_u)))
                blocks = iter(range(DECODE_BLOCKS))

                def next_lo():
                    j = next(blocks)
                    n = FIRST_U + PICK_TURNS * PICK_BLOCKS + RING + j
                    split_lo(i * DECODE_BLOCKS + n, n % RING)

                for w, keys in enumerate((key1, key2)):
                    next_lo()
                    link(e.tensor_tensor(hit, iota[:, None, 0:PTOP].to_broadcast([P, HK, PTOP]),
                                         ranks[:, w, :, None].to_broadcast([P, HK, PTOP]), ALU.is_equal))
                    next_lo()
                    k4 = keys.rearrange("p a n -> p (a n)")[:, at].rearrange("p (h r) -> p h r", h=PEER_H)
                    h4 = hit.rearrange("p (h k) r -> p h k r", h=PEER_H)
                    link(e.tensor_tensor(h4, h4, k4[:, :, None, :].to_broadcast([P, PEER_H, PTOP, PTOP]), ALU.mult))
                    next_lo()
                    ins = e.tensor_reduce(sel[:, w, :][:, at], hit, AX_X, ALU.add)
                    if w:
                        ins.then_inc(decoded, 1)
                        e.wait_ge(decoded, i + 1)
                    else:
                        link(ins)
                    next_lo()
            assert steps[0] == DECODE_LINKS, steps
            base[0], steps[0] = start + TH * DECODE_LINKS, 0
            e.wait_ge(pick_exp, 1)
            g3 = sel[:, 2, :].rearrange("p (h k) -> p h k", k=PTOP)
            link(e.tensor_reduce(gsum[:], g3, AX_X, ALU.add))
            link(e.reciprocal(gsum[:], gsum[:]))
            e.tensor_tensor(g3, g3, gsum[:, :, None].to_broadcast([P, TH * PEER_H, PTOP]),
                            ALU.mult).then_inc(sel_rows, 1)
            e.wait_ge(sel_T, 1)
            e.tensor_copy(sel[:, 0:2, :], ps[:, 4, :].rearrange("p (a t) -> p a t", a=2))
            link(e.tensor_copy(sel[:, 2, :], ps[:, 5, 0:T]))

            def hot(half, g, s, first=False):
                if not first:
                    e.wait_ge(hot_used, g + (half * GROUPS - 1))
                at = bass.ds(g * GROUP, GROUP)
                e.tensor_tensor(hot_l[s], iota[:, None, :].to_broadcast([P, GROUP, P]),
                                sel[:, 0, :][:, at][:, :, None].to_broadcast([P, GROUP, P]), ALU.is_equal)
                keys = iota[:, None, KEYS_H * half:KEYS_H * half + KEYS_H]
                e.tensor_tensor(hot_k[s], keys.to_broadcast([P, GROUP, KEYS_H]),
                                sel[:, 1, :][:, at][:, :, None].to_broadcast([P, GROUP, KEYS_H]),
                                ALU.is_equal).then_inc(hot_ready, 1)

            acts = act[:].rearrange("p (i t) -> p i t", t=T)

            def weigh(half, g, s):
                e.wait_ge(hot_used, g + (half * GROUPS + 1))
                v = acts[:, KEYS_H * half:KEYS_H * half + KEYS_H, bass.ds(g * GROUP, GROUP)]
                bank = s + (0 if half else 6)
                e.tensor_tensor(v, ps[:, bank, 0:GROUP * KEYS_H].rearrange("p (t i) -> p i t", t=GROUP), v,
                                ALU.mult).then_inc(gates_used, 1)

            def expert_lo(i2, slot):
                e.wait_ge(wexp_hi, i2 + 1)
                e.tensor_tensor(h_lo[:, slot, :], act[:, bass.ds(i2 * T, T)], h_hi[:, slot, :].bitcast(F32),
                                ALU.subtract).then_inc(wexp_lo, 1)

            e.wait_ge(x_stored, 16)
            e.wait_ge(gelu_ready, NKEYS - GROUPS)
            first = FIRST_U + NKEYS - GROUPS + RING

            def gate_round(i, last=False):
                for j in range(RING):
                    split_lo(i * RING + (first + j), (first + j) % RING)
                    weigh(0, i * RING + j, j % 2)
                    if last and j >= RING - 2:
                        hot(1, j - (RING - 2), j % 2)
                    else:
                        hot(0, i * RING + (j + 2), j % 2)

            rounds = GROUPS // RING
            for s in range(2):
                hot(0, s, s, first=True)
            with e.Fori(0, rounds - 1) as i:
                gate_round(i)
            gate_round(rounds - 1, last=True)
            for j in range(RING):
                expert_lo(j, j)
            e.wait_ge(gelu_ready, NKEYS)
            for g in range(RING):
                weigh(1, g, g % 2)
                hot(1, g + 2, g % 2)

            def mix_round(i, last=False):
                for j in range(RING):
                    n = FIRST_V + RING + j
                    split_lo(i * RING + n, n % RING)
                    expert_lo(i * RING + (RING + j), j)
                    weigh(1, i * RING + (RING + j), j % 2)
                    if not (last and j >= RING - 2):
                        hot(1, i * RING + (RING + j + 2), j % 2)

            n_first = (NKEYS - GROUPS) // RING - 1
            with e.Fori(0, n_first - 1) as i:
                mix_round(i)
            mix_round(n_first - 1, last=True)
            with e.Fori(n_first, NKEYS // RING - 1) as i:
                for j in range(RING):
                    n = FIRST_V + RING + j
                    split_lo(i * RING + n, n % RING)
                    expert_lo(i * RING + (RING + j), j)
            e.wait_ge(x_loaded, 32)
            e.wait_ge(block_used, FIRST_V + NKEYS)
            for c in range(KC):
                e.scalar_tensor_tensor(out=x[:, c, :], in0=ps[:, 4 + c // 2, (c % 2) * T:(c % 2) * T + T],
                                       scalar=mod[:, 5 * KC + c:5 * KC + c + 1], in1=x[:, c, :],
                                       op0=ALU.mult, op1=ALU.add).then_inc(out_added, 1)
            norm(2)
            norm_end(2)
            for c in range(KC):
                ins = e.scalar_tensor_tensor(out=norm_fin[:, c, :], in0=x[:, c, :], scalar=gain[:, 2, c:c + 1],
                                             in1=rstd, op0=ALU.mult, op1=ALU.mult)
                if c % 2:
                    ins.then_inc(out_ready, 1)

        @block.tensor
        def _(e):
            def product(out, a, b, start, stop, check=True):
                (a_hi, a_lo), (b_hi, b_lo) = a, b
                e.matmul(out, a_hi, b_hi, start=start, stop=False, skip_group_check=not check)
                e.matmul(out, a_hi, b_lo, start=False, stop=False, skip_group_check=not check)
                return e.matmul(out, a_lo, b_hi, start=False, stop=stop, skip_group_check=not check)

            def columns(n, slot, out):
                e.wait_ge(lo_ready, n + 1)
                for k in range(KC):
                    last = product(out, (w_hi[slot][:, k, :], w_lo[slot][:, k, :]),
                                   (h_hi[:, k, :], h_lo[:, k, :]), k == 0, k == KC - 1)
                last.then_inc(block_used, 1)

            def rows(n, blocks, out):
                slot = n % RING
                width = P * blocks
                e.wait_ge(lo_ready, n + blocks)
                for b in range(TH):
                    cols = slice(P * b, P * b + P)
                    o = out[:, 256 * b:256 * b + width].rearrange("p (a m) -> p a m", a=blocks)
                    for k in range(KC):
                        last = product(o, (h_hi[:, k, cols], h_lo[:, k, cols]),
                                       (all_hi[:, slot:slot + blocks, k, :], all_lo[:, slot:slot + blocks, k, :]),
                                       k == 0, k == KC - 1)
                last.then_inc(block_used, blocks)

            def first_blocks(n, outs, wait):
                for k in range(KC // 2):
                    wait(k)
                    for s in range(RING):
                        if k == 0:
                            e.wait_ge(lo_ready, n + s + 1)
                        slot, (out, start) = (n + s) % RING, outs[s]
                        product(out, (w_hi[slot][:, k, :], w_lo[slot][:, k, :]), (h_hi[:, k, :], h_lo[:, k, :]),
                                k == 0 and start, False, check=False)
                for s in range(RING):
                    slot, (out, _) = (n + s) % RING, outs[s]
                    for k in range(KC // 2, KC):
                        if s == 0:
                            wait(k)
                        last = product(out, (w_hi[slot][:, k, :], w_lo[slot][:, k, :]), (h_hi[:, k, :], h_lo[:, k, :]),
                                       False, k == KC - 1, check=False)
                    last.then_inc(block_used, 1)

            def mean_squares(i, a=0, z=KC):
                for k in range(a, z):
                    e.wait_ge(squares, i * KC + k + 1)
                    last = e.matmul(ps[:, mean_bank(i), 0:T], mean_w, norm_a[:, k, :], start=(k == 0),
                                    stop=(k == KC - 1))
                if z == KC:
                    last.then_inc(mean_ready, 1)

            def index_scores(b):
                S = P * (b + 1)
                if b == 0:
                    e.wait_ge(evac_v, evac[2][1])
                else:
                    e.wait_ge(relu_ready, 4 * b)
                for h in range(8):
                    g, a = h % 4, h // 4
                    rowg = slice(32 * g, 32 * g + 32)
                    for z in range(2):
                        last = e.matmul(ps[:, 4 + g, 256 * a:256 * a + S], qi[rowg, a, z, P * b:P * b + P],
                                        ki[rowg, z, 0:S], start=(z == 0), stop=(z == 1))
                last.then_inc(isc_ready, 1)

            def logits(b):
                S = P * (b + 1)
                if b == 0:
                    e.wait_ge(evac_v, evac[9][1])
                    e.wait_ge(relu_ready, 8)
                else:
                    e.wait_ge(probT_copied, 1)
                for h in range(8):
                    g, a = h % 4, h // 4
                    rowg = slice(32 * g, 32 * g + 32)
                    for z in range(2):
                        last = e.matmul(ps[:, 4 + g, 256 * a:256 * a + S], qa[rowg, a, z, P * b:P * b + P],
                                        ka[rowg, a, z, 0:S], start=(z == 0), stop=(z == 1))
                last.then_inc(logit_ready, 1)

            def turn_probs(b):
                e.wait_ge(prob_ready, b + 1)
                for ck in range(b + 1):
                    for k in range(8):
                        last = e.transpose(ps[:, 4 + 2 * ck + k // 4, P * (k % 4):P * (k % 4) + P],
                                           prob[:, k, P * ck:P * ck + P], ident)
                last.then_inc(probT_ready, 1)

            def attend(b):
                e.wait_ge(probT_copied, (b + 1) * (b + 2) // 2)
                if b:
                    e.wait_ge(att_copied, b)
                for h in range(8):
                    k = 2 * (h % 4) + h // 4
                    out = ps[64 * (h % 2):64 * (h % 2) + 64, 3, P * (h // 2):P * (h // 2) + P]
                    for ck in range(b + 1):
                        last = e.matmul(out, va[:, ck, 64 * h:64 * h + 64], probT[:, ck, k, :],
                                        start=(ck == 0), stop=(ck == b))
                last.then_inc(att_ready, 1)

            def retention_scores():
                e.wait_ge(evac_v, evac[14][1])
                for r in range(RET_H):
                    tile, rg = r // 2, slice(64 * (r % 2), 64 * (r % 2) + 64)
                    for first, width, jc in ((0, 256, 0), (256, 128, 1)):
                        for z in range(2):
                            last = e.matmul(ps[:, 4 + r, first:first + width], kr[rg, tile, z, P * jc:P * jc + P],
                                            qr[rg, tile, z, P * jc:T], start=(z == 0), stop=(z == 1))
                last.then_inc(inner_ready, 1)

            def retain():
                e.wait_ge(inner_used, 1)
                e.wait_ge(evac_s, n_evac_s)
                for r in range(RET_H):
                    out = ps[:, 4 + r // 2, 256 * (r % 2):256 * (r % 2) + 256]
                    e.matmul(out, vr[:, 0, P * r:P * r + P], inner[:, r, 0:256], start=True, stop=False,
                             skip_group_check=True)
                    last = e.matmul(out[:, P:T], vr[:, 1, P * r:P * r + P], inner[:, r, 256:384], start=False,
                                    stop=True, skip_group_check=True)
                last.then_inc(ret_ready, 1)

            def group_mean(src, done):
                flat = src.rearrange("p h t -> p (h t)")
                for c in range(2):
                    last = e.matmul(ps[:, 6 + c, :], mean_w, flat[:, 512 * c:512 * c + 512], start=True, stop=True)
                last.then_inc(done, 1)

            e.wait_ge(kept_loaded, 16)
            mean_squares(0)
            first_blocks(0, [(proj_bank(s // 2)[:, 256 * (s % 2):256 * (s % 2) + 256], s % 2 == 0) for s in range(RING)],
                         lambda k: e.wait_ge(h_ready, k + 1))
            for n in range(RING, N_IN):
                q = pair_of[n]
                kind, blocks = PAIRS[q][1:]
                if half_of[n] == 0 and q >= PROJ_BANKS:
                    e.wait_ge(*evac[q - PROJ_BANKS])
                if kind != ROWS:
                    columns(n, n % RING, proj_bank(q)[:, 256 * half_of[n]:256 * half_of[n] + 256])
                elif half_of[n] == 0:
                    rows(n, blocks, proj_bank(q))
                for b in range(TH):
                    if n == INDEX_AFTER[b]:
                        index_scores(b)
                    if n == PROBT_AFTER[b]:
                        turn_probs(b)
                    if n == ATT_AFTER[b]:
                        attend(b)
                    if n == LOGITS_AFTER[b]:
                        logits(b)
                if n == INNER_AFTER:
                    retention_scores()
                if n == RET_AFTER:
                    retain()
            e.wait_ge(ret_copied, 1)
            group_mean(ro, gmean_ready)

            def mixed_chunk(k):
                if k == 0:
                    e.wait_ge(mix_ready, 1)
                if k == KC // 2:
                    e.wait_ge(centred, 1)
                    group_mean(rsq, gvar_ready)
                    e.wait_ge(mix_ready, 2)

            e.wait_ge(evac_v, n_evac_v)
            first_blocks(FIRST_OUT, [(ps[:, s, 0:T], True) for s in range(RING)], mixed_chunk)
            for c in range(RING, N_OUT):
                n = FIRST_OUT + c
                e.wait_ge(out_added, c - 3)
                columns(n, n % RING, ps[:, c % 4, 0:T])
                mean_squares(1, c - RING, c - RING + 1)
            mean_squares(1, RING, KC)
            e.wait_ge(out_added, KC)
            first_blocks(FIRST_PQ, [(ps[:, s, 0:T], True) for s in range(RING)],
                         lambda k: e.wait_ge(h_ready, KC + k + 1))
            for c in range(RING, N_PQ):
                e.wait_ge(qry_copied, c - 3)
                n = FIRST_PQ + c
                columns(n, n % RING, ps[:, c % 4, 0:T])

            def scores(b):
                if b:
                    e.wait_ge(score_copied, b)
                for c in range(N_PQ):
                    last = e.matmul(ps[:, 4 + c // 4, P * (c % 4):P * (c % 4) + P], qry[:, c, P * b:P * b + P],
                                    sk[:, c, :], start=True, stop=True)
                last.then_inc(score_ready, 1)

            e.wait_ge(sk_loaded, 16)
            for j in range(RING):
                e.wait_ge(qry_copied, N_PQ - RING + j + 1)
                columns(FIRST_U + j, (FIRST_U + j) % RING, ps[:, j, 0:T])
                if j < TH:
                    e.wait_ge(qry_copied, N_PQ)
                    scores(j)
            def expert_block(i, j):
                e.wait_ge(gelu_ready, i * RING + (j - RING + 1))
                columns(i * RING + (FIRST_U + j), (FIRST_U + j) % RING, ps[:, j, 0:T])

            n_first = (NKEYS - GROUPS) // RING
            with e.Fori(1, n_first) as i:
                for j in range(RING):
                    expert_block(i, j)

            e.wait_ge(sel_rows, 1)
            for w in range(3):
                for b in range(TH):
                    last = e.transpose(ps[:, 4 + w // 2, (w % 2) * T + P * b:(w % 2) * T + P * b + P],
                                       sel[:, w, P * b:P * b + P], ident)
            last.then_inc(sel_T, 1)

            def gate_rows(g, s, half, first=False):
                e.wait_ge(gated, g + 1)
                if not first:
                    e.wait_ge(gates_used, g - 1)
                for t in range(GROUP):
                    last = e.matmul(ps[:, s + (0 if half else 6), KEYS_H * t:KEYS_H * t + KEYS_H], hot_l[s][:, t, :],
                                    hot_r[s][:, t, :], start=True, stop=True)
                last.then_inc(hot_used, 1)

            for j in range(RING):
                expert_block(n_first, j)
                gate_rows(j, j % 2, 0, first=j < 2)
            with e.Fori(1, GROUPS // RING) as i:
                for j in range(RING):
                    expert_block(i + n_first, j)
                    gate_rows(i * RING + j, j % 2, 0)
            e.wait_ge(gelu_ready, NKEYS)
            for g in range(RING):
                gate_rows(GROUPS + g, g % 2, 1)

            def mix_experts(i2, j, start, stop):
                slot = (FIRST_V + j) % RING
                e.wait_ge(wexp_lo, i2 + 1)
                e.wait_ge(lo_ready, i2 + (FIRST_V + 1))
                for c in range(KC):
                    last = product(ps[:, 4 + c // 2, (c % 2) * T:(c % 2) * T + T],
                                   (w_hi[slot][:, c, :], w_lo[slot][:, c, :]),
                                   (h_hi[:, j, :], h_lo[:, j, :]), start and c % 2 == 0, stop, check=False)
                last.then_inc(block_used, 1)

            for j in range(RING):
                mix_experts(j, j, j == 0, False)
                gate_rows(GROUPS + RING + j, j % 2, 1)
            with e.Fori(1, n_first - 1) as i:
                for j in range(RING):
                    mix_experts(i * RING + j, j, False, False)
                    gate_rows(i * RING + (GROUPS + RING + j), j % 2, 1)
            with e.Fori(n_first - 1, NKEYS // RING - 1) as i:
                for j in range(RING):
                    mix_experts(i * RING + j, j, False, False)
            for j in range(RING):
                mix_experts(NKEYS - RING + j, j, False, j == RING - 1)
            mean_squares(2)


def _rope_tables():
    t = np.arange(T, dtype=np.float32)

    def cs(inv, copies):
        ang = t[None, :] * inv[:, None]
        c = np.tile(np.cos(ang), (copies, 1)).astype(np.float32)
        s = np.tile(np.sin(ang), (copies, 1)).astype(np.float32)
        return [c, s, s, c]

    att = (1.0 / (np.float32(10000.0) ** (np.arange(0, ATT_D, 2, dtype=np.float32) / ATT_D))).astype(np.float32)
    ret = (1.0 / (np.float32(10000.0) ** np.linspace(0.0, 1.0, RET_D // 2, dtype=np.float32))).astype(np.float32)
    log_g = np.log(1.0 - 2.0 ** (-5.0 - np.arange(RET_H, dtype=np.float64)))
    diff = np.arange(T)[None, :] - np.arange(P)[:, None]
    decay = [np.where(diff >= 0, np.exp(g * np.maximum(diff, 0)), 0.0) * RET_D ** -0.5 for g in log_g]
    causal = np.where(np.arange(P)[None, :] <= np.arange(P)[:, None], 0.0, NEG)
    tab = np.concatenate(cs(att, 4) + cs(ret, 2) + decay + [causal], axis=1).astype(np.float32)
    keep = np.stack([np.tile(np.arange(P), (P, 1)), np.eye(P), np.full((P, P), 1.0 / P)], axis=1).astype(np.float32)
    return np.ascontiguousarray(tab), np.ascontiguousarray(keep)


def _blocks(w):
    n = w.shape[1] // P
    return w.reshape(KC, P, n, P).transpose(2, 1, 0, 3).reshape(n, P, KC * P)


def _in_columns():
    at = dict(qa=0, ka=512, va=1024, qi=1536, ki=2048, wi=2112, qr=2120, kr=2632, vr=3144, gr=3656)
    out = []
    for name, kind, _ in PAIRS:
        base, i = at[name[:2]], int(name[2:] or 0)
        if name == "wi":
            out += [base + c for c in range(ATT_H)] + [-1] * (P - ATT_H)
        elif kind != ROT:
            out += range(base + 256 * i, base + 256 * i + 256)
        else:
            heads, half = (2, 64) if name[1] == "r" else (4, 32)
            for z in range(2):
                for g in range(heads):
                    head = 0 if name == "ki" else heads * i + g
                    out += [base + head * 2 * half + z * half + j for j in range(half)]
    return np.array(out)


def kernel(x, c, w_ada, b_ada, norm_mix_g, w_in, w_out, norm_ffn_g, w_pq, sub_keys, u_emb, v_emb, norm_final_g):
    import concourse.bacc as bacc
    from concourse.bass_utils import run_bass_kernel_spmd as run

    x, c, w_ada, b_ada, norm_mix_g, w_in, w_out, norm_ffn_g, w_pq, sub_keys, u_emb, v_emb, norm_final_g = (
        np.asarray(a) for a in (x, c, w_ada, b_ada, norm_mix_g, w_in, w_out, norm_ffn_g, w_pq, sub_keys,
                                u_emb, v_emb, norm_final_g))

    def columns(v):
        return v.reshape(-1, P).T

    tab, keep = _rope_tables()
    cols = _in_columns()
    w_cols = np.concatenate([w_in[0], np.zeros((D, 1), np.float32)], axis=1)[:, cols]
    arrays = {
        "xT": x[0].reshape(T, KC, P).transpose(2, 1, 0),
        "c_rows": np.broadcast_to(c[0], (P, D)),
        "w_ada": w_ada[0].T.reshape(ADA_LOADS, ADA_GROUP, P, D).transpose(0, 2, 1, 3).reshape(ADA_LOADS, P, -1),
        "b_ada": columns(b_ada[0]),
        "gains": np.stack([columns(norm_mix_g[0]), columns(norm_ffn_g[0]), columns(norm_final_g)], axis=1),
        "tables": tab,
        "keep": keep,
        "early": np.concatenate([_blocks(w_cols), _blocks(w_out[0]), _blocks(w_pq[0])]),
        "skeys": sub_keys[0].reshape(2 * PEER_H, NKEYS, P).transpose(2, 0, 1),
        "u": u_emb[0].reshape(NKEYS, NKEYS, KC, P).transpose(1, 3, 2, 0).reshape(NKEYS, P, KC * P),
        "v": v_emb[0].reshape(NKEYS, NKEYS, D).transpose(1, 0, 2),
    }
    nc = bacc.Bacc("TRN2", target_bir_lowering=False, num_devices=1)
    sent, args = {}, []
    for name, a in arrays.items():
        sent[name] = np.ascontiguousarray(a)
        args.append(nc.dram_tensor(name, a.shape, F32, kind="ExternalInput").ap())
    args.append(nc.dram_tensor("outT", (P, KC, T), F32, kind="ExternalOutput").ap())
    build(nc, *args)
    r = run(nc, [sent], core_ids=[0])
    y = np.asarray(r.results[0]["outT"])
    return np.ascontiguousarray(y.transpose(2, 1, 0).reshape(1, T, D))
```

```python
from contextlib import ExitStack
from functools import partial

import numpy as np

import concourse.bass as bass
from concourse import mybir

F32 = mybir.dt.float32
F32R = mybir.dt.float32r
U32 = mybir.dt.uint32
BF16 = mybir.dt.bfloat16
ALU = mybir.AluOpType
ACT = mybir.ActivationFunctionType
AX_X = mybir.AxisListType.X

P = 128
D = 1024
KC = D // P
T = 256
TH = T // P
ATT_H, ATT_D = 8, 64
RET_H, RET_D = 4, 128
TOPK = min(256, T // 4)
PEER_H, NKEYS, PTOP = 8, 128, 16
EPS = 1e-6
N_MOD = 6
EARLY_PICKS = 2
PICK_BLOCKS = 8
DECODE_BLOCKS = 8
PICK_LINKS = 11
TAKEN_AT = 5
DECODE_LINKS = 15
HK = PEER_H * PTOP
KEYS_H = NKEYS // 2
PARTS = 3
GROUP = 4
GROUPS = T // GROUP

ROT = "rotate"
ROWS = "rows"
GATE = "gate"
PAIRS = [("ki", ROT, 2), ("qi0", ROT, 2), ("qi1", ROT, 2), ("wi", ROWS, 1),
         ("ka0", ROT, 2), ("va0", ROWS, 2), ("ka1", ROT, 2), ("va1", ROWS, 2), ("qa0", ROT, 2), ("qa1", ROT, 2),
         ("kr0", ROT, 2), ("kr1", ROT, 2), ("qr0", ROT, 2), ("vr0", ROWS, 2), ("qr1", ROT, 2), ("vr1", ROWS, 2),
         ("gr0", GATE, 2), ("gr1", GATE, 2)]
PROJ_BANKS = 3
INDEX_AMONG = (9, 12)
LOGITS_AMONG = (21, 25)
PROBT_AFTER = (23, 28)
ATT_AFTER = (25, 30)
INNER_AMONG = 32
RET_AFTER = 33
INDEX_AT = (13, 16)
PICK_AT = ((14, 15), (17, 18, 19, 20, 21, 22, 23))
SOFTMAX_AT = (23, 27)
EXP_AT = (24, 29)
NORMAL_AT = (24, 29)
PROBT_AT = (25, 32)
ATT_AT = (29, 33)
INNER_AT = 34
RET_AT = 36
ADA_AT = (5, 7, 8, 9, 10, 11, 13, 14, 25, 26, 27, 30, 32, 33, 35, 36)
N_IN = sum(p[2] for p in PAIRS)
N_OUT = KC
N_PQ = 2 * PEER_H
FIRST_OUT = N_IN
FIRST_PQ = FIRST_OUT + N_OUT
N_EARLY = FIRST_PQ + N_PQ
FIRST_U = N_EARLY
FIRST_V = FIRST_U + NKEYS
RING = 4
ADA_GROUP = 2
N_ADA = N_MOD * KC
ADA_LOADS = N_ADA // ADA_GROUP
ADA_RING = 4
ADA_FIRST = 8
BIAS_GROUP = 4
NEG = -1.0e30
TAKEN = -3.0e38

TAB = dict(att_cs=(0, 512), att_sc=(512, 1024), ret_cs=(1024, 1536), ret_sc=(1536, 2048),
           decay=(2048, 3072), causal=(3072, 3200))
TAB_W = 3200


def build(nc, xT, cb, ada_first, ada, ada_b, gains, tables, keep, early, skeys, uw, vw, outT):
    with ExitStack() as ctx:
        def sb(name, shape, dt=F32):
            return ctx.enter_context(nc.sbuf_tensor(name, shape, dt))

        def sem(name):
            return ctx.enter_context(nc.semaphore(name))

        act = sb("act", [P, NKEYS * T])
        h_hi = sb("h_hi", [P, KC, T], F32R)
        h_lo = sb("h_lo", [P, KC, T], F32R)
        x = sb("x", [P, KC, T])
        raw = [sb(f"raw{s}", [P, KC * P]) for s in range(RING)]
        all_hi = sb("w_hi", [P, RING, KC, P], F32R)
        all_lo = sb("w_lo", [P, RING, KC, P], F32R)
        w_hi = [all_hi[:, s] for s in range(RING)]
        w_lo = [all_lo[:, s] for s in range(RING)]
        kept = sb("kept", [P, 3, P])
        iota, ident, mean_w = kept[:, 0, :], kept[:, 1, :], kept[:, 2, :]
        sel = sb("sel", [P, 3, T])
        mod = sb("mod", [P, N_ADA])
        mod_b = sb("mod_b", [P, N_ADA])
        gain = sb("gain", [P, 3, KC])
        gmod = sb("gmod", [P, 2, KC])
        gsum = sb("gsum", [P, TH * PEER_H])

        x_flat = x[:].rearrange("p k t -> p (k t)")
        x_half = x_flat.bitcast(BF16)

        def halves(at, n):
            return x_half[:, at:at + n]

        L, R = GROUP * NKEYS, GROUP * KEYS_H
        wide_iota = halves(0, L).rearrange("p (i t) -> p i t", t=GROUP)
        hot_l = [halves(L * (1 + s), L).rearrange("p (i t) -> p i t", t=GROUP) for s in range(2)]
        hot_k = [halves(3 * L + R * s, R).rearrange("p (i t) -> p i t", t=GROUP) for s in range(2)]
        hot_r = [halves(3 * L + R * (2 + PARTS * s), PARTS * R).rearrange("p (c i t) -> p c i t", c=PARTS, t=GROUP)
                 for s in range(2)]
        gate_rest = x_flat[:, D * TH - T:D * TH]
        assert 3 * L + R * (2 + 2 * PARTS) <= 2 * (D * TH - T)
        sel_half = sel[:].rearrange("p a t -> p (a t)").bitcast(BF16)
        keys_t = sel_half[:, 0:2 * T].rearrange("p (a t) -> p a t", a=2)
        gates_t = sel_half[:, 2 * T:(2 + PARTS) * T].rearrange("p (a t) -> p a t", a=PARTS)

        top = [0]

        def scratch(*dims, at=None):
            n = int(np.prod(dims))
            if at is None:
                at = top[0]
                top[0] += n
            assert at + n <= NKEYS * T, (at, n)
            v = act[:, at:at + n]
            if len(dims) == 2:
                v = v.rearrange("p (a b) -> p a b", a=dims[0])
            elif len(dims) == 3:
                v = v.rearrange("p (a b c) -> p a b c", a=dims[0], b=dims[1])
            return v

        ada_ring = scratch(ADA_RING, ADA_GROUP, D)
        c_row = scratch(D)
        c_col = scratch(KC)
        c_tmp = scratch(KC)
        tab = scratch(TAB_W)
        rot_a = scratch(2, T)
        rot_b = scratch(2, T)
        more_ada = scratch(ADA_FIRST - ADA_RING, ADA_GROUP, D, at=top[0])
        ka = scratch(2, 2, T)
        qa = scratch(2, 2, T)
        qi = scratch(2, 2, T)
        ki = scratch(2, T)
        kr = scratch(2, 2, T)
        qr = scratch(2, 2, T)
        gr = scratch(4, T)
        va = scratch(TH, 512)
        vr = scratch(TH, 512)
        wi = scratch(TH, 8)
        att_o = scratch(4, T)
        isc = scratch(TH, T)
        best = scratch(8)
        mask = scratch(TH, T)
        inner = scratch(RET_H, 384)
        rmax = scratch(8)
        rsum = scratch(8)
        rinv = scratch(8)
        shared = top[0]
        norm_fin = scratch(KC, T, at=0)
        norm_a = scratch(KC, T, at=shared)
        norm_b = scratch(KC, T, at=shared + 2048)
        relu = scratch(8, T, at=shared)
        prob = scratch(8, T, at=shared)
        probT = scratch(2, 8, P, at=shared + 2048)
        rstd = scratch(T, at=shared + 4096)
        ro = scratch(4, T, at=shared + 4096 + 256)
        rsq = scratch(4, T, at=shared + 5120 + 256)
        assert shared + 6400 <= NKEYS * T
        top[0] = NKEYS * T // 2
        qry = scratch(2 * PEER_H, T)
        sk = scratch(2 * PEER_H, NKEYS)
        score = scratch(TH, PEER_H, 2 * NKEYS)
        wk = [scratch(2, NKEYS) for _ in range(2)]
        val = [scratch(2, PTOP) for _ in range(2)]
        idx = [scratch(2, PTOP) for _ in range(2)]
        cand = [scratch(PTOP * PTOP) for _ in range(2)]
        cval = [scratch(PTOP) for _ in range(2)]
        cpos = [scratch(PTOP) for _ in range(2)]
        top_p = scratch(TH, HK)
        rank_u = scratch(HK)
        keys_h = scratch(2 * TH * HK // 2).bitcast(BF16).rearrange("p (w b r) -> p w b r", w=2, b=TH)
        rank_h = scratch(HK).bitcast(BF16).rearrange("p (w m) -> p w m", w=2)
        wide_rank = scratch(PTOP * HK // 2).bitcast(BF16).rearrange("p (r m) -> p r m", r=PTOP)
        hit = scratch(PTOP * HK // 2).bitcast(BF16).rearrange("p (r m) -> p r m", r=PTOP)
        assert top[0] <= NKEYS * T, top[0]

        def u32(ap):
            return ap.bitcast(U32)

        def tb(name):
            return tab[:, TAB[name][0]:TAB[name][1]]

        ps = ctx.enter_context(nc.psum_tensor("ps", [P, 8, 512], F32))

        x_loaded = sem("x_loaded")
        c_loaded = sem("c_loaded")
        small_loaded = sem("small_loaded")
        tab_loaded = sem("tab_loaded")
        more_tab_loaded = sem("more_tab_loaded")
        kept_loaded = sem("kept_loaded")
        sk_loaded = sem("sk_loaded")
        ada_loaded = [sem(f"ada_loaded{n}") for n in range(ADA_FIRST)]
        ada_more = [sem(f"ada_more{s}") for s in range(ADA_RING)]
        raw_loaded = [sem(f"raw_loaded{s}") for s in range(RING)]
        hi_ready = sem("hi_ready")
        lo_ready = sem("lo_ready")
        block_used = sem("block_used")
        c_exp = sem("c_exp")
        c_silu = sem("c_silu")
        c_spread = sem("c_spread")
        c_ready = sem("c_ready")
        ada_used = sem("ada_used")
        affine = sem("affine")
        squares = sem("squares")
        mean_ready = sem("mean_ready")
        mean_eps = sem("mean_eps")
        root_ready = sem("root_ready")
        normed = sem("normed")
        h_hi_ready = sem("h_hi_ready")
        h_ready = sem("h_ready")
        chain = sem("chain")
        evac_v = sem("evac_v")
        evac_s = sem("evac_s")
        gate_exp = sem("gate_exp")
        isc_ready = sem("isc_ready")
        relu_ready = sem("relu_ready")
        relu_used = sem("relu_used")
        logit_ready = sem("logit_ready")
        logit_used = sem("logit_used")
        shifted = sem("shifted")
        exp_ready = sem("exp_ready")
        prob_ready = sem("prob_ready")
        probT_ready = sem("probT_ready")
        probT_copied = sem("probT_copied")
        att_ready = sem("att_ready")
        att_copied = sem("att_copied")
        mix_hi = sem("mix_hi")
        inner_ready = sem("inner_ready")
        inner_used = sem("inner_used")
        ret_ready = sem("ret_ready")
        ret_copied = sem("ret_copied")
        gmean_ready = sem("gmean_ready")
        centred = sem("centred")
        squared = sem("squared")
        gvar_ready = sem("gvar_ready")
        gstd_ready = sem("gstd_ready")
        spread_ready = sem("spread_ready")
        gvar_eps = sem("gvar_eps")
        groot = sem("groot")
        ret_done = sem("ret_done")
        ret_hi = sem("ret_hi")
        mix_ready = sem("mix_ready")
        out_added = sem("out_added")
        qry_copied = sem("qry_copied")
        score_ready = sem("score_ready")
        score_copied = sem("score_copied")
        gelu_ready = sem("gelu_ready")
        searches = sem("searches")
        pick_step = [sem(f"pick_step{h}") for h in range(2)]
        picked = sem("picked")
        decoded = sem("decoded")
        pick_exp = sem("pick_exp")
        sel_T = sem("sel_T")
        score_taken = sem("score_taken")
        x_stored = sem("x_stored")
        keys_hot = sem("keys_hot")
        hot_ready = sem("hot_ready")
        hot_used = sem("hot_used")
        gates_used = sem("gates_used")
        mixed = sem("mixed")
        wexp_hi = sem("wexp_hi")
        wexp_lo = sem("wexp_lo")
        out_ready = sem("out_ready")
        stored = sem("stored")

        block = ctx.enter_context(nc.Block())

        evac = []
        nv = ns = 0
        for _, kind, _ in PAIRS:
            if kind == ROWS:
                ns += 1
                evac.append((evac_s, ns))
            else:
                nv += 1
                evac.append((evac_v, nv))
        n_evac_v, n_evac_s = nv, ns
        pair_of, half_of, last_of = [], [], []
        for q, (_, _, blocks) in enumerate(PAIRS):
            for i in range(blocks):
                pair_of.append(q)
                half_of.append(i)
            last_of.append(len(pair_of) - 1)

        def ada_slot(n):
            return n if n < ADA_FIRST else n % ADA_RING

        def ada_place(n):
            slot = ada_slot(n)
            return ada_ring[:, slot] if slot < ADA_RING else more_ada[:, slot - ADA_RING]

        def ada_there(n):
            if n < ADA_FIRST:
                return ada_loaded[n], 16
            return ada_more[n % ADA_RING], 16 * ((n - ADA_FIRST) // ADA_RING + 1)

        def mean_bank(i):
            return 0 if i == 2 else 7

        def proj_bank(q):
            return ps[:, q % PROJ_BANKS, :]

        @block.sync
        def _(sp):
            sp.dma_start(c_col, cb).then_inc(c_loaded, 16)
            sp.dma_start(kept[:], keep).then_inc(kept_loaded, 16)

            def load(source, slot):
                sp.dma_start(raw[slot][:], source).then_inc(raw_loaded[slot], 16)

            sp.dma_start(x[:], xT).then_inc(x_loaded, 16)
            for s in range(RING):
                load(early[s], s)
            for k in range(ADA_FIRST):
                sp.dma_start(ada_place(k).rearrange("p g k -> p (g k)"), ada_first[k]).then_inc(ada_loaded[k], 16)
            first = TAB["att_sc"][1]
            rounds = N_EARLY // RING
            for s in range(RING):
                sp.wait_ge(lo_ready, s + 1)
                load(early[RING + s], s)
                if s == 0:
                    sp.dma_start(tab[:, 0:first], tables[:, 0:first]).then_inc(tab_loaded, 16)
            sp.dma_start(tab[:, first:], tables[:, first:]).then_inc(more_tab_loaded, 16)
            with sp.Fori(2, rounds) as i:
                for s in range(RING):
                    sp.wait_ge(lo_ready, i * RING + s - RING + 1)
                    sp.dma_start(raw[s][:], early[bass.ds(i * RING + s, 1)].rearrange("a p n -> (a p) n")
                                 ).then_inc(raw_loaded[s], 16)
            for n in range(rounds * RING, N_EARLY):
                sp.wait_ge(lo_ready, n - RING + 1)
                load(early[n], n % RING)
            sp.wait_ge(out_added, KC)
            sp.dma_start(outT, x[:]).then_inc(x_stored, 16)
            for first, source in ((FIRST_U, uw), (FIRST_V, vw)):
                with sp.Fori(0, NKEYS // RING) as i:
                    for j in range(RING):
                        s = (first + j) % RING
                        sp.wait_ge(lo_ready, i * RING + (first + j - RING + 1))
                        sp.dma_start(raw[s][:], source[bass.ds(i * RING + j, 1)].rearrange("a p n -> (a p) n")
                                     ).then_inc(raw_loaded[s], 16)
            sp.wait_ge(gates_used, 2 * GROUPS)
            sp.wait_ge(x_stored, 16)
            sp.dma_start(x[:], outT).then_inc(x_loaded, 16)
            for c in range(4):
                sp.wait_ge(out_ready, c + 1)
                sp.dma_start(outT[:, c * KC // 4:(c + 1) * KC // 4, :],
                             norm_fin[:, c * KC // 4:(c + 1) * KC // 4, :]).then_inc(stored, 16)
            sp.wait_ge(stored, 64)

        @block.gpsimd
        def _(pool):
            pool.dma_start(mod_b[:], ada_b).then_inc(small_loaded, 16)
            pool.dma_start(gain[:], gains).then_inc(small_loaded, 16)
            for n in range(ADA_FIRST, ADA_LOADS):
                before = n - (ADA_RING if n - ADA_RING >= ADA_FIRST else ADA_FIRST)
                pool.wait_ge(ada_used, (before + 1) * ADA_GROUP)
                pool.wait_ge(lo_ready, RING + ADA_GROUP * (n - ADA_FIRST))
                pool.dma_start(ada_place(n).rearrange("p g k -> p (g k)"), ada[n - ADA_FIRST]).then_inc(ada_more[n % ADA_RING], 16)
            pool.wait_ge(out_added, KC)
            pool.dma_start(sk, skeys).then_inc(sk_loaded, 16)


        @block.scalar
        def _(e):
            def split_hi(n, slot, turn):
                e.wait_ge(raw_loaded[slot], turn * 16)
                if not isinstance(n, int) or n >= RING:
                    e.wait_ge(block_used, n - RING + 1)
                e.activation(w_hi[slot], raw[slot][:].rearrange("p (k m) -> p k m", k=KC),
                             ACT.Copy).then_inc(hi_ready, 1)

            def square(i, k):
                if i:
                    e.wait_ge(out_added, (i - 1) * KC + k + 1)
                e.activation(norm_a[:, k, :], x[:, k, :], ACT.Square).then_inc(squares, 1)

            def root(i):
                e.wait_ge(mean_eps, i + 1)
                e.activation(rstd, rstd, ACT.Sqrt).then_inc(root_ready, 1)

            def ffn_norm_hi():
                at = 3 * KC
                for k in range(KC):
                    e.wait_ge(normed, KC + k + 1)
                    e.activation(h_hi[:, k, :], norm_b[:, k, :], ACT.Identity,
                                 bias=mod[:, at + k:at + k + 1]).then_inc(h_hi_ready, 1)

            e.wait_ge(c_loaded, 16)
            e.activation(c_tmp, c_col, ACT.Exp, scale=-1.0).then_inc(c_exp, 1)
            e.wait_ge(c_spread, 1)
            e.activation(c_row, ps[:, 0:2, :].rearrange("p a b -> p (a b)"), ACT.Copy).then_inc(c_ready, 1)
            e.wait_ge(x_loaded, 16)
            for k in range(KC):
                square(0, k)
            for n in range(RING):
                split_hi(n, n, 1)
            root(0)
            e.wait_ge(normed, KC)
            for k in range(KC):
                e.wait_ge(ada_used, ADA_GROUP * (k + 1))
                e.activation(norm_b[:, k, :], norm_a[:, k, :], ACT.Identity, scale=gmod[:, 0, k:k + 1],
                             bias=mod[:, k:k + 1]).then_inc(affine, 1)
                e.wait_ge(affine, k + 1)
                e.activation(h_hi[:, k, :], norm_b[:, k, :], ACT.Copy).then_inc(h_hi_ready, 1)

            def take(q):
                name, kind, _ = PAIRS[q]
                e.wait_ge(block_used, last_of[q] + 1)
                src = proj_bank(q)
                if kind == GATE:
                    i = int(name[-1])
                    if q + 1 == len(PAIRS):
                        e.wait_ge(evac_v, n_evac_v - 1)
                        e.activation(rot_a.rearrange("p a b -> p (a b)"), src, ACT.Copy)
                    e.activation(gr[:, 2 * i:2 * i + 2, :], src.rearrange("p (a b) -> p a b", a=2), ACT.Exp,
                                 scale=-1.0).then_inc(gate_exp, 1)
                elif name == "wi":
                    e.activation(wi, src.rearrange("p (a b) -> p a b", a=TH)[:, :, 0:8], ACT.Copy,
                                 scale=float(ATT_H) ** -0.5).then_inc(evac_s, 1)
                else:
                    i = int(name[-1])
                    dst = (va if name[1] == "a" else vr)[:, :, 256 * i:256 * i + 256]
                    e.activation(dst, src.rearrange("p (t c) -> p t c", t=TH), ACT.Copy).then_inc(evac_s, 1)

            def index_relu(b):
                S = P * (b + 1)
                e.wait_ge(isc_ready, b + 1)
                if b:
                    e.wait_ge(relu_used, b)
                for g in range(4):
                    e.activation(relu[:, 2 * g:2 * g + 2, 0:S],
                                 ps[:, 4 + g, :].rearrange("p (a s) -> p a s", a=2)[:, :, 0:S], ACT.Relu,
                                 scale=0.125).then_inc(relu_ready, 1)

            def softmax_exp(b):
                e.wait_ge(shifted, b + 1)
                for h in range(8):
                    e.activation(prob[:, h, 0:P * (b + 1)], prob[:, h, 0:P * (b + 1)], ACT.Exp, bias=rmax[:, h:h + 1],
                                 accum_out=rsum[:, h:h + 1]).then_inc(exp_ready, 1)

            def take_probT(b):
                e.wait_ge(probT_ready, b + 1)
                for ck in range(b + 1):
                    e.activation(probT[:, ck].rearrange("p (a h) t -> p a h t", a=2),
                                 ps[:, 4 + 2 * ck:6 + 2 * ck, :].rearrange("p a (h t) -> p a h t", h=4), ACT.Copy
                                 ).then_inc(probT_copied, 1)

            def take_att(b):
                e.wait_ge(att_ready, b + 1)
                e.activation(att_o[:, :, P * b:P * b + P], ps[:, 3, :].rearrange("p (a t) -> p a t", a=4),
                             ACT.Copy).then_inc(att_copied, 1)

            for n in range(RING, N_IN + RING):
                split_hi(n, n % RING, n // RING + 1)
                if n - 3 < N_IN and n - 3 == last_of[pair_of[n - 3]] and PAIRS[pair_of[n - 3]][1] != ROT:
                    take(pair_of[n - 3])
                for b in range(TH):
                    if n == INDEX_AT[b]:
                        index_relu(b)
                    if n == PROBT_AT[b]:
                        take_probT(b)
                    if n == ATT_AT[b]:
                        take_att(b)
                    if n == EXP_AT[b]:
                        softmax_exp(b)
                if n == RET_AT:
                    e.wait_ge(ret_ready, 1)
                    e.activation(ro, ps[:, 4:6, :].rearrange("p a (b t) -> p (a b) t", b=2),
                                 ACT.Copy).then_inc(ret_copied, 1)
            e.wait_ge(block_used, N_IN)
            e.wait_ge(att_copied, TH)
            e.activation(h_hi[:, 0:4, :], att_o, ACT.Copy).then_inc(mix_hi, 1)
            e.wait_ge(centred, 1)
            e.activation(rsq, ro, ACT.Square).then_inc(squared, 1)
            e.wait_ge(gvar_eps, 1)
            e.activation(rstd, rstd, ACT.Sqrt).then_inc(groot, 1)
            for r in range(RET_H):
                e.wait_ge(ret_done, r + 1)
                e.activation(h_hi[:, 4 + r, :], ro[:, r, :], ACT.Copy).then_inc(ret_hi, 1)
            for c in range(KC):
                n = FIRST_OUT + RING + c
                if c < RING:
                    split_hi(n, n % RING, n // RING + 1)
                square(1, c)
                if c >= RING:
                    split_hi(n, n % RING, n // RING + 1)
                if c == RING:
                    e.preload_act_table(ACT.Sqrt)
            root(1)
            ffn_norm_hi()

            def take_query(i):
                e.wait_ge(block_used, FIRST_PQ + i + 1)
                e.activation(qry[:, i, :], ps[:, i % 4, 0:T], ACT.Copy).then_inc(qry_copied, 1)

            def take_score(h):
                e.wait_ge(score_ready, h + 1)
                e.activation(score[:, :, h, :], ps[:, 4 + h % 4, :].rearrange("p (b n) -> p b n", b=TH),
                             ACT.Copy).then_inc(score_copied, 1)

            def copy_score(h):
                if isinstance(h, int):
                    e.wait_ge(score_copied, h + 1)
                for b in range(TH):
                    if not isinstance(h, int) or h:
                        e.wait_ge(pick_step[b], h * PICK_LINKS + (TAKEN_AT - PICK_LINKS))
                    e.activation(wk[b].rearrange("p a n -> p (a n)"),
                                 score[:, b].rearrange("p h n -> p (h n)")[:, bass.ds(h * (2 * NKEYS), 2 * NKEYS)],
                                 ACT.Copy).then_inc(score_taken, 1)

            for n in range(FIRST_PQ + RING, N_EARLY + RING):
                split_hi(n, n % RING, n // RING + 1)
                i = n - FIRST_PQ - RING
                take_query(i)
                if i >= 5 and i % 2:
                    take_score((i - 5) // 2)
                if i == 5:
                    copy_score(0)
                if i == 10:
                    copy_score(1)
            take_score(PEER_H - 2)
            copy_score(2)
            take_score(PEER_H - 1)
            e.wait_ge(ada_used, N_ADA)
            e.preload_act_table(ACT.Gelu)

            def gelu(n, i2, bank):
                e.wait_ge(block_used, n + 1)
                e.activation(act[:, bass.ds(i2 * T, T)], ps[:, bank, 0:T], ACT.Gelu).then_inc(gelu_ready, 1)

            def expert_round(i, blocks, first, before=lambda j: None):
                for j in range(blocks):
                    n = FIRST_U + first + RING + j
                    before(j)
                    split_hi(i * blocks + n, n % RING, i * (blocks // RING) + (n // RING + 1))
                    gelu(i * blocks + (n - RING), i * blocks + (first + j), (first + j) % RING)

            turns = PEER_H - EARLY_PICKS
            e.wait_ge(score_copied, PEER_H)
            with e.Fori(0, turns - 1) as i:
                expert_round(i, PICK_BLOCKS, 0,
                             before=lambda j: copy_score(i + (EARLY_PICKS + 1)) if j == TAKEN_AT else None)
            expert_round(turns - 1, PICK_BLOCKS, 0)
            e.wait_ge(picked, TH * PEER_H)
            e.activation(sel[:, 2, :], sel[:, 2, :], ACT.Exp).then_inc(pick_exp, 1)
            e.preload_act_table(ACT.Gelu)
            first = turns * PICK_BLOCKS
            with e.Fori(0, TH) as i:
                expert_round(i, DECODE_BLOCKS, first)
            e.wait_ge(decoded, TH)
            with e.Fori(0, GROUPS // RING) as i:
                expert_round(i, RING, NKEYS - GROUPS)

            def expert_hi(i2, slot):
                e.activation(h_hi[:, slot, :], act[:, bass.ds(i2 * T, T)], ACT.Copy).then_inc(wexp_hi, 1)

            e.wait_ge(gates_used, GROUPS)
            for j in range(RING):
                expert_hi(j, j)

            def mix_round(i):
                for j in range(RING):
                    n = FIRST_V + RING + j
                    split_hi(i * RING + n, n % RING, i + (n // RING + 1))
                    expert_hi(i * RING + (RING + j), j)

            n_first = (NKEYS - GROUPS) // RING - 1
            with e.Fori(0, n_first) as i:
                mix_round(i)
            e.wait_ge(gates_used, 2 * GROUPS)
            with e.Fori(n_first, NKEYS // RING - 1) as i:
                mix_round(i)
            e.preload_act_table(ACT.Sqrt)
            for k in range(KC):
                square(2, k)
            root(2)

        @block.vector
        def _(e):
            base, steps = [0], [0]

            def link(ins, search=False):
                steps[0] += 1
                ins.then_inc(chain, 1)
                e.wait_ge(chain, base[0] + steps[0])
                if search:
                    e.sem_inc(searches, 1)

            def split_lo(n, slot):
                e.wait_ge(hi_ready, n + 1)
                e.tensor_tensor(w_lo[slot], raw[slot][:].rearrange("p (k m) -> p k m", k=KC),
                                w_hi[slot].bitcast(F32), ALU.subtract).then_inc(lo_ready, 1)

            def ada_block(m):
                load = m // ADA_GROUP
                e.wait_ge(*ada_there(load))
                w = ada_place(load)[:, m % ADA_GROUP, :]
                e.tensor_tensor_reduce(w, w, c_row, 1.0, 0.0, ALU.mult, ALU.add,
                                       mod[:, m:m + 1]).then_inc(ada_used, 1)
                if m % BIAS_GROUP == BIAS_GROUP - 1:
                    a = m + 1 - BIAS_GROUP
                    e.wait_ge(ada_used, m + 1)
                    link(e.tensor_tensor(mod[:, a:m + 1], mod[:, a:m + 1], mod_b[:, a:m + 1], ALU.add))

            def ffn_gain():
                link(e.scalar_tensor_tensor(out=gmod[:, 1, :], in0=mod[:, 4 * KC:5 * KC], scalar=1.0,
                                            in1=gain[:, 1, :], op0=ALU.add, op1=ALU.mult))

            def norm(i):
                e.wait_ge(mean_ready, i + 1)
                e.tensor_scalar(rstd, ps[:, mean_bank(i), 0:T], 1.0 / KC, EPS, ALU.mult, ALU.add).then_inc(mean_eps, 1)

            def norm_end(i):
                e.wait_ge(root_ready, i + 1)
                link(e.reciprocal(rstd, rstd))

            def ffn_norm():
                at = 3 * KC
                for k in range(KC + 1):
                    if k < KC:
                        e.scalar_tensor_tensor(out=norm_b[:, k, :], in0=x[:, k, :], scalar=gmod[:, 1, k:k + 1],
                                               in1=rstd, op0=ALU.mult, op1=ALU.mult).then_inc(normed, 1)
                    if k:
                        e.wait_ge(h_hi_ready, KC + k)
                        e.scalar_tensor_tensor(out=h_lo[:, k - 1, :], in0=norm_b[:, k - 1, :],
                                               scalar=mod[:, at + k - 1:at + k], in1=h_hi[:, k - 1, :].bitcast(F32),
                                               op0=ALU.add, op1=ALU.subtract).then_inc(h_ready, 1)

            e.wait_ge(c_exp, 1)
            link(e.tensor_scalar(c_tmp, c_tmp, 1.0, None, ALU.add))
            link(e.reciprocal(c_tmp, c_tmp))
            e.tensor_tensor(c_col, c_col, c_tmp, ALU.mult).then_inc(c_silu, 1)
            e.wait_ge(small_loaded, 32)
            for n in range(RING):
                split_lo(n, n)
                if n == 1:
                    norm(0)
            norm_end(0)
            e.tensor_tensor(norm_a, x[:], rstd[:, None, :].to_broadcast([P, KC, T]), ALU.mult).then_inc(normed, KC)
            e.wait_ge(c_ready, 1)
            for k in range(KC + 1):
                if k < KC:
                    e.wait_ge(ada_loaded[k], 16)
                    for z in range(2):
                        w = ada_place(k)[:, z, :]
                        ins = e.tensor_tensor_reduce(w, w, c_row, 1.0, 0.0, ALU.mult, ALU.add,
                                                     mod[:, z * KC + k:z * KC + k + 1])
                    link(ins)
                    pair = slice(k, 2 * KC, KC)
                    link(e.tensor_tensor(mod[:, pair], mod[:, pair], mod_b[:, pair], ALU.add))
                    e.scalar_tensor_tensor(out=gmod[:, 0, k:k + 1], in0=mod[:, KC + k:KC + k + 1], scalar=1.0,
                                           in1=gain[:, 0, k:k + 1], op0=ALU.add,
                                           op1=ALU.mult).then_inc(ada_used, ADA_GROUP)
                if k:
                    e.wait_ge(h_hi_ready, k)
                    e.tensor_tensor(h_lo[:, k - 1, :], norm_b[:, k - 1, :], h_hi[:, k - 1, :].bitcast(F32),
                                    ALU.subtract).then_inc(h_ready, 1)

            dest = dict(ki=(ki,), qi=(qi[:, 0], qi[:, 1]), ka=(ka[:, 0], ka[:, 1]), qa=(qa[:, 0], qa[:, 1]),
                        kr=(kr[:, 0], kr[:, 1]), qr=(qr[:, 0], qr[:, 1]))

            def rotate(q):
                name = PAIRS[q][0]
                out = dest[name[:2]][int(name[2:] or 0)]
                kind = "ret" if name[1] == "r" else "att"
                e.wait_ge(block_used, last_of[q] + 1)
                pair = proj_bank(q)
                e.tensor_tensor(rot_a.rearrange("p a b -> p (a b)"), pair, tb(kind + "_cs"), ALU.mult)
                link(e.tensor_tensor(rot_b.rearrange("p a b -> p (a b)"), pair, tb(kind + "_sc"), ALU.mult))
                e.tensor_tensor(out[:, 0, :], rot_a[:, 0, :], rot_a[:, 1, :], ALU.subtract)
                last = e.tensor_tensor(out[:, 1, :], rot_b[:, 0, :], rot_b[:, 1, :], ALU.add)
                last.then_inc(evac_v, 1)
                e.wait_ge(evac_v, evac[q][1])

            def gate(q):
                i = int(PAIRS[q][0][-1])
                g = gr[:, 2 * i:2 * i + 2, :]
                e.wait_ge(gate_exp, i + 1)
                link(e.tensor_scalar(g, g, 1.0, None, ALU.add))
                link(e.reciprocal(g, g))
                src = rot_a if q + 1 == len(PAIRS) else proj_bank(q).rearrange("p (a b) -> p a b", a=2)
                e.tensor_tensor(g, src, g, ALU.mult).then_inc(evac_v, 1)
                e.wait_ge(evac_v, evac[q][1])

            def index_sum(b):
                S = P * (b + 1)
                if b == 0:
                    e.wait_ge(evac_s, evac[3][1])
                for k in range(8):
                    g, tile = k // 2, k % 2
                    h = 4 * tile + g
                    e.wait_ge(relu_ready, 4 * b + g + 1)
                    if k == 0:
                        link(e.tensor_scalar(isc[:, b, 0:S], relu[:, k, 0:S], wi[:, b, h:h + 1], None, ALU.mult))
                    else:
                        ins = e.scalar_tensor_tensor(out=isc[:, b, 0:S], in0=relu[:, k, 0:S], scalar=wi[:, b, h:h + 1],
                                                     in1=isc[:, b, 0:S], op0=ALU.mult, op1=ALU.add)
                        if k == 7:
                            ins.then_inc(relu_used, 1)
                            e.wait_ge(relu_used, b + 1)
                        else:
                            link(ins)
                diag = isc[:, b, P * b:P * b + P]
                link(e.tensor_tensor(diag, diag, tb("causal"), ALU.add))

            def index_pick(b, a, z):
                S = P * (b + 1)
                s = isc[:, b, 0:S]
                for _ in range(a, z):
                    link(e.max(best, s))
                    link(e.match_replace(s, best, s, TAKEN))

            def index_mask(b):
                S = P * (b + 1)
                link(e.tensor_scalar(mask[:, b, 0:S], isc[:, b, 0:S], 0.5 * TAKEN, NEG, ALU.is_gt, ALU.mult))
                diag = mask[:, b, P * b:P * b + P]
                link(e.tensor_tensor(diag, diag, tb("causal"), ALU.add))

            e.wait_ge(tab_loaded, 16)
            def softmax_in(b):
                S = P * (b + 1)
                e.wait_ge(logit_ready, b + 1)
                m = mask[:, b, 0:S]
                src = ps[:, 4:8, :].rearrange("p g (a s) -> p (g a) s", a=2)[:, :, 0:S]
                e.scalar_tensor_tensor(out=prob[:, :, 0:S], in0=src, scalar=float(ATT_D) ** -0.5,
                                       in1=m[:, None, :].to_broadcast([P, 8, S]), op0=ALU.mult,
                                       op1=ALU.add).then_inc(logit_used, 1)
                e.wait_ge(logit_used, b + 1)
                link(e.tensor_reduce(rmax, prob[:, :, 0:S], AX_X, ALU.max))
                e.tensor_scalar(rmax, rmax, -1.0, None, ALU.mult).then_inc(shifted, 1)

            def softmax_out(b):
                S = P * (b + 1)
                e.wait_ge(exp_ready, 8 * (b + 1))
                link(e.reciprocal(rinv, rsum))
                e.tensor_tensor(prob[:, :, 0:S], prob[:, :, 0:S], rinv[:, :, None].to_broadcast([P, 8, S]),
                                ALU.mult).then_inc(prob_ready, 1)
                e.wait_ge(prob_ready, b + 1)

            ada_next = 2 * KC
            for n in range(RING, N_IN + RING):
                split_lo(n, n % RING)
                if n == last_of[9] + 3:
                    e.wait_ge(more_tab_loaded, 16)
                if n - 3 < N_IN and n - 3 == last_of[pair_of[n - 3]]:
                    q = pair_of[n - 3]
                    if PAIRS[q][1] == ROT:
                        rotate(q)
                    elif PAIRS[q][1] == GATE and q + 1 < len(PAIRS):
                        gate(q)
                for b in range(TH):
                    if n == INDEX_AT[b]:
                        index_sum(b)
                    if n in PICK_AT[b]:
                        k, rounds = PICK_AT[b].index(n), TOPK // 8
                        index_pick(b, rounds * k // len(PICK_AT[b]), rounds * (k + 1) // len(PICK_AT[b]))
                        if n == PICK_AT[b][-1]:
                            index_mask(b)
                    if n == SOFTMAX_AT[b]:
                        softmax_in(b)
                    if n == NORMAL_AT[b]:
                        softmax_out(b)
                if n == INNER_AT:
                    e.wait_ge(inner_ready, 1)
                    for r in range(RET_H):
                        pr = ps[:, 4 + r, 0:384]
                        dec_r = tb("decay").rearrange("p (r t) -> p r t", r=RET_H)[:, r, :]
                        e.tensor_tensor(inner[:, r, 0:256], pr[:, 0:256], dec_r, ALU.mult)
                        last = e.tensor_tensor(inner[:, r, 256:384], pr[:, 256:384], dec_r[:, 0:P], ALU.mult)
                    last.then_inc(inner_used, 1)
                if n in ADA_AT:
                    ada_block(ada_next)
                    ada_next += 1

            e.wait_ge(mix_hi, 1)
            e.tensor_tensor(h_lo[:, 0:4, :], att_o, h_hi[:, 0:4, :].bitcast(F32), ALU.subtract).then_inc(mix_ready, 1)
            e.wait_ge(ret_copied, 1)
            e.wait_ge(gmean_ready, 1)
            e.tensor_tensor(ro, ro, ps[:, 6:8, :].rearrange("p a (b t) -> p (a b) t", b=2),
                            ALU.subtract).then_inc(centred, 1)
            gate(len(PAIRS) - 1)
            e.wait_ge(gvar_ready, 1)
            e.tensor_scalar(rstd, ps[:, 6, 0:T], EPS, None, ALU.add).then_inc(gvar_eps, 1)
            e.wait_ge(centred, 1)
            e.wait_ge(groot, 1)
            e.reciprocal(rstd, rstd).then_inc(gstd_ready, 1)
            link(e.tensor_tensor(ro, ro, gr, ALU.mult))
            ada_block(ada_next)
            ada_next += 1
            scaled = False
            e.wait_ge(spread_ready, 1)
            for r in range(RET_H + 1):
                if r < RET_H:
                    e.scalar_tensor_tensor(out=ro[:, r, :], in0=ro[:, r, :], scalar=float(RET_H),
                                           in1=ps[:, 4 + r, 0:T], op0=ALU.mult,
                                           op1=ALU.mult).then_inc(ret_done, 1)
                if r:
                    e.wait_ge(ret_hi, r)
                    e.tensor_tensor(h_lo[:, 3 + r, :], ro[:, r - 1, :], h_hi[:, 3 + r, :].bitcast(F32),
                                    ALU.subtract).then_inc(mix_ready, 1)

            def add_out(c):
                e.wait_ge(block_used, FIRST_OUT + c + 1)
                e.scalar_tensor_tensor(out=x[:, c, :], in0=ps[:, c % 4, 0:T], scalar=mod[:, 2 * KC + c:2 * KC + c + 1],
                                       in1=x[:, c, :], op0=ALU.mult, op1=ALU.add).then_inc(out_added, 1)

            for c in range(KC):
                n = FIRST_OUT + RING + c
                if c < RING:
                    split_lo(n, n % RING)
                add_out(c)
                if ada_next < 5 * KC:
                    ada_block(ada_next)
                    ada_next += 1
                if c > RING:
                    split_lo(n - 1, (n - 1) % RING)
                if ada_next == 5 * KC and not scaled:
                    ffn_gain()
                    scaled = True
            assert scaled
            split_lo(n, n % RING)
            norm(1)
            norm_end(1)
            ffn_norm()
            def pick(k, split):
                both = range(TH)

                def step(b, n):
                    e.wait_ge(pick_step[b], k * PICK_LINKS + n)

                def search(b, n):
                    step(b, n)
                    e.sem_inc(searches, 1)

                for b in both:
                    e.wait_ge(score_taken, k * TH + (b + 1))
                    e.sem_inc(searches, 1)
                    e.max(val[b][:, 0, 0:8], wk[b][:, 0, :])
                    e.max(val[b][:, 1, 0:8], wk[b][:, 1, :]).then_inc(pick_step[b], 1)
                for b in both:
                    search(b, 1)
                    e.max_index(u32(idx[b][:, 0, 0:8]), val[b][:, 0, 0:8], wk[b][:, 0, :])
                    e.max_index(u32(idx[b][:, 1, 0:8]), val[b][:, 1, 0:8], wk[b][:, 1, :]).then_inc(pick_step[b], 1)
                split(0)
                for b in both:
                    search(b, 2)
                    e.match_replace(wk[b][:, 0, :], val[b][:, 0, 0:8], wk[b][:, 0, :], TAKEN)
                    e.match_replace(wk[b][:, 1, :], val[b][:, 1, 0:8], wk[b][:, 1, :], TAKEN).then_inc(pick_step[b], 1)
                split(1)
                for b in both:
                    search(b, 3)
                    e.max(val[b][:, 0, 8:16], wk[b][:, 0, :])
                    e.max(val[b][:, 1, 8:16], wk[b][:, 1, :]).then_inc(pick_step[b], 1)
                split(2)
                for b in both:
                    search(b, 4)
                    e.max_index(u32(idx[b][:, 0, 8:16]), val[b][:, 0, 8:16], wk[b][:, 0, :])
                    e.max_index(u32(idx[b][:, 1, 8:16]), val[b][:, 1, 8:16], wk[b][:, 1, :]).then_inc(pick_step[b], 1)
                split(3)
                for b in both:
                    step(b, TAKEN_AT)
                    e.tensor_tensor(cand[b].rearrange("p (a b) -> p a b", a=PTOP),
                                    val[b][:, 0, :, None].to_broadcast([P, PTOP, PTOP]),
                                    val[b][:, 1, None, :].to_broadcast([P, PTOP, PTOP]),
                                    ALU.add).then_inc(pick_step[b], 1)
                for b in both:
                    search(b, 6)
                    e.max(cval[b][:, 0:8], cand[b]).then_inc(pick_step[b], 1)
                split(4)
                for b in both:
                    search(b, 7)
                    e.max_index(u32(cpos[b][:, 0:8]), cval[b][:, 0:8], cand[b]).then_inc(pick_step[b], 1)
                split(5)
                for b in both:
                    search(b, 8)
                    e.match_replace(cand[b], cval[b][:, 0:8], cand[b], TAKEN).then_inc(pick_step[b], 1)
                split(6)
                for b in both:
                    search(b, 9)
                    e.max(cval[b][:, 8:16], cand[b]).then_inc(pick_step[b], 1)
                for b in both:
                    search(b, 10)
                    e.max_index(u32(cpos[b][:, 8:16]), cval[b][:, 8:16], cand[b]).then_inc(pick_step[b], 1)
                split(7)
                head = bass.ds(k, 1)
                for b in both:
                    step(b, PICK_LINKS)
                    e.tensor_scalar(sel[:, 2, :][:, bass.ds(k * PTOP + b * HK, PTOP)], cval[b], cval[b][:, 0:1], None,
                                    ALU.subtract)
                    for w in range(2):
                        e.tensor_copy(keys_h[:, w, b, :].rearrange("p (r h) -> p r h", r=PTOP)[:, :, head],
                                      u32(idx[b][:, w, :])[:, :, None])
                    e.tensor_copy(u32(top_p[:, b, :]).rearrange("p (r h) -> p r h", r=PTOP)[:, :, head],
                                  u32(cpos[b])[:, :, None]).then_inc(picked, 1)
                e.wait_ge(picked, k * TH + TH)

            at = iter(range(FIRST_PQ + RING, N_EARLY + RING))

            def split_next(_=None):
                n = next(at)
                split_lo(n, n % RING)

            for _ in range(6):
                split_next()
                for _ in range(2):
                    if ada_next < N_ADA:
                        ada_block(ada_next)
                        ada_next += 1
            assert ada_next == N_ADA
            for k in range(EARLY_PICKS):
                pick(k, lambda n: split_next() if n in (0, 2, 3, 5, 7) else None)
            turns = PEER_H - EARLY_PICKS
            with e.Fori(0, turns) as i:
                def split(j):
                    n = FIRST_U + RING + j
                    split_lo(i * PICK_BLOCKS + n, n % RING)

                pick(i + EARLY_PICKS, split)

            e.tensor_copy(wide_rank, iota[:, 0:PTOP, None].to_broadcast([P, PTOP, HK]))
            e.wait_ge(x_stored, 16)
            e.tensor_copy(wide_iota, iota[:, :, None].to_broadcast([P, NKEYS, GROUP]))
            e.wait_ge(pick_exp, 1)
            g3 = sel[:, 2, :].rearrange("p (h k) -> p h k", k=PTOP)
            link(e.tensor_reduce(gsum[:], g3, AX_X, ALU.add))
            link(e.reciprocal(gsum[:], gsum[:]))
            link(e.tensor_tensor(g3, g3, gsum[:, :, None].to_broadcast([P, TH * PEER_H, PTOP]), ALU.mult))
            start = base[0] + steps[0]
            with e.Fori(0, TH) as i:
                base[0], steps[0] = i * DECODE_LINKS + start, 0
                pos = u32(top_p.rearrange("p a n -> p (a n)"))[:, bass.ds(i * HK, HK)]
                for w, (op, arg) in enumerate(((ALU.logical_shift_right, 4), (ALU.bitwise_and, 15))):
                    link(e.tensor_scalar(u32(rank_u), pos, arg, None, op))
                    link(e.tensor_copy(rank_h[:, w, :], u32(rank_u)))
                blocks = iter(range(DECODE_BLOCKS))

                def next_lo():
                    n = FIRST_U + turns * PICK_BLOCKS + RING + next(blocks)
                    split_lo(i * DECODE_BLOCKS + n, n % RING)

                for w in range(2):
                    next_lo()
                    link(e.tensor_tensor(hit, wide_rank, rank_h[:, w, None, :].to_broadcast([P, PTOP, HK]),
                                         ALU.is_equal))
                    next_lo()
                    hits = hit.rearrange("p r (k h) -> p r k h", h=PEER_H)
                    keys = keys_h[:, w].rearrange("p b m -> p (b m)")[:, bass.ds(i * HK, HK)].rearrange(
                        "p (r h) -> p r h", h=PEER_H)
                    link(e.tensor_tensor(hits, hits, keys[:, :, None, :].to_broadcast([P, PTOP, PTOP, PEER_H]), ALU.mult))
                    next_lo()
                    for rows in (8, 4, 2):
                        link(e.tensor_tensor(hit[:, 0:rows, :], hit[:, 0:rows, :], hit[:, rows:2 * rows, :], ALU.add))
                    next_lo()
                    out = sel[:, w, :][:, bass.ds(i * HK, HK)].rearrange("p (h k) -> p k h", h=PEER_H)
                    ins = e.tensor_tensor(out, hit[:, 0, :].rearrange("p (k h) -> p k h", h=PEER_H),
                                          hit[:, 1, :].rearrange("p (k h) -> p k h", h=PEER_H), ALU.add)
                    if w:
                        ins.then_inc(decoded, 1)
                        e.wait_ge(decoded, i + 1)
                    else:
                        link(ins)
            assert steps[0] == DECODE_LINKS, steps
            base[0], steps[0] = start + TH * DECODE_LINKS, 0
            e.wait_ge(sel_T, 1)
            e.tensor_copy(keys_t, ps[:, 4, :].rearrange("p (a t) -> p a t", a=2))
            rest = ps[:, 5, 0:T]
            for part in range(PARTS):
                link(e.tensor_copy(gates_t[:, part, :], rest))
                if part + 1 < PARTS:
                    link(e.tensor_tensor(gate_rest, rest, gates_t[:, part, :], ALU.subtract))
                rest = gate_rest

            def hot(half, g, s, first=False):
                if not first:
                    e.wait_ge(hot_used, g + (half * GROUPS - 1))
                at = bass.ds(g * GROUP, GROUP)
                e.tensor_tensor(hot_l[s], wide_iota, keys_t[:, 0, :][:, at][:, None, :].to_broadcast([P, NKEYS, GROUP]),
                                ALU.is_equal)
                e.tensor_tensor(hot_k[s], wide_iota[:, KEYS_H * half:KEYS_H * half + KEYS_H, :],
                                keys_t[:, 1, :][:, at][:, None, :].to_broadcast([P, KEYS_H, GROUP]),
                                ALU.is_equal).then_inc(keys_hot, 1)
                e.wait_ge(keys_hot, g + (half * GROUPS + 1))
                e.tensor_tensor(hot_r[s], hot_k[s][:, None, :, :].to_broadcast([P, PARTS, KEYS_H, GROUP]),
                                gates_t[:, :, at][:, :, None, :].to_broadcast([P, PARTS, KEYS_H, GROUP]),
                                ALU.mult).then_inc(hot_ready, 1)

            acts = act[:].rearrange("p (i t) -> p i t", t=T)

            def weigh(half, g, s):
                e.wait_ge(hot_used, g + (half * GROUPS + 1))
                v = acts[:, KEYS_H * half:KEYS_H * half + KEYS_H, bass.ds(g * GROUP, GROUP)]
                bank = s + (0 if half else 6)
                e.tensor_tensor(v, ps[:, bank, 0:GROUP * KEYS_H].rearrange("p (t i) -> p i t", t=GROUP), v,
                                ALU.mult).then_inc(gates_used, 1)

            def expert_lo(i2, slot):
                e.wait_ge(wexp_hi, i2 + 1)
                e.tensor_tensor(h_lo[:, slot, :], act[:, bass.ds(i2 * T, T)], h_hi[:, slot, :].bitcast(F32),
                                ALU.subtract).then_inc(wexp_lo, 1)

            e.wait_ge(gelu_ready, NKEYS - GROUPS)
            first = FIRST_U + NKEYS - GROUPS + RING

            def gate_round(i, last=False):
                for j in range(RING):
                    split_lo(i * RING + (first + j), (first + j) % RING)
                    weigh(0, i * RING + j, j % 2)
                    if last and j >= RING - 2:
                        hot(1, j - (RING - 2), j % 2)
                    else:
                        hot(0, i * RING + (j + 2), j % 2)

            rounds = GROUPS // RING
            for s in range(2):
                hot(0, s, s, first=True)
            with e.Fori(0, rounds - 1) as i:
                gate_round(i)
            gate_round(rounds - 1, last=True)
            for j in range(RING):
                expert_lo(j, j)
            e.wait_ge(gelu_ready, NKEYS)
            for g in range(RING):
                weigh(1, g, g % 2)
                hot(1, g + 2, g % 2)

            def mix_round(i, last=False):
                for j in range(RING):
                    n = FIRST_V + RING + j
                    split_lo(i * RING + n, n % RING)
                    expert_lo(i * RING + (RING + j), j)
                    weigh(1, i * RING + (RING + j), j % 2)
                    if not (last and j >= RING - 2):
                        hot(1, i * RING + (RING + j + 2), j % 2)

            n_first = (NKEYS - GROUPS) // RING - 1
            with e.Fori(0, n_first - 1) as i:
                mix_round(i)
            mix_round(n_first - 1, last=True)
            with e.Fori(n_first, NKEYS // RING - 1) as i:
                for j in range(RING):
                    n = FIRST_V + RING + j
                    split_lo(i * RING + n, n % RING)
                    expert_lo(i * RING + (RING + j), j)
            e.wait_ge(x_loaded, 32)
            for c in range(KC):
                e.wait_ge(mixed, c // 2 + 1)
                e.scalar_tensor_tensor(out=x[:, c, :], in0=ps[:, 4 + c // 2, (c % 2) * T:(c % 2) * T + T],
                                       scalar=mod[:, 5 * KC + c:5 * KC + c + 1], in1=x[:, c, :],
                                       op0=ALU.mult, op1=ALU.add).then_inc(out_added, 1)
            norm(2)
            norm_end(2)
            for c in range(KC):
                ins = e.scalar_tensor_tensor(out=norm_fin[:, c, :], in0=x[:, c, :], scalar=gain[:, 2, c:c + 1],
                                             in1=rstd, op0=ALU.mult, op1=ALU.mult)
                if c % 2:
                    ins.then_inc(out_ready, 1)

        @block.tensor
        def _(e):
            def product(out, a, b, start, stop, check=True):
                (a_hi, a_lo), (b_hi, b_lo) = a, b
                e.matmul(out, a_hi, b_hi, start=start, stop=False, skip_group_check=not check)
                e.matmul(out, a_hi, b_lo, start=False, stop=False, skip_group_check=not check)
                return e.matmul(out, a_lo, b_hi, start=False, stop=stop, skip_group_check=not check)

            def columns(n, slot, out, among=None):
                e.wait_ge(lo_ready, n + 1)
                for k in range(KC):
                    last = product(out, (w_hi[slot][:, k, :], w_lo[slot][:, k, :]),
                                   (h_hi[:, k, :], h_lo[:, k, :]), k == 0, k == KC - 1)
                    if k == KC - 1:
                        last.then_inc(block_used, 1)
                    if among:
                        among(k)

            def rows(n, blocks, out, among=None):
                slot = n % RING
                width = P * blocks
                e.wait_ge(lo_ready, n + blocks)
                for b in range(TH):
                    cols = slice(P * b, P * b + P)
                    o = out[:, 256 * b:256 * b + width].rearrange("p (a m) -> p a m", a=blocks)
                    for k in range(KC):
                        last = product(o, (h_hi[:, k, cols], h_lo[:, k, cols]),
                                       (all_hi[:, slot:slot + blocks, k, :], all_lo[:, slot:slot + blocks, k, :]),
                                       k == 0, k == KC - 1)
                        if among and b == 0:
                            among(k)
                last.then_inc(block_used, blocks)

            def first_blocks(n, outs, wait, whole=False):
                for k in range(KC if whole else KC // 2):
                    wait(k)
                    for s in range(RING):
                        if k == 0:
                            e.wait_ge(lo_ready, n + s + 1)
                        slot, (out, start) = (n + s) % RING, outs[s]
                        last = product(out, (w_hi[slot][:, k, :], w_lo[slot][:, k, :]), (h_hi[:, k, :], h_lo[:, k, :]),
                                       k == 0 and start, k == KC - 1, check=False)
                        if k == KC - 1:
                            last.then_inc(block_used, 1)
                if whole:
                    return
                for s in range(RING):
                    slot, (out, _) = (n + s) % RING, outs[s]
                    for k in range(KC // 2, KC):
                        if s == 0:
                            wait(k)
                        last = product(out, (w_hi[slot][:, k, :], w_lo[slot][:, k, :]), (h_hi[:, k, :], h_lo[:, k, :]),
                                       False, k == KC - 1, check=False)
                    last.then_inc(block_used, 1)

            def mean_squares(i, a=0, z=KC):
                for k in range(a, z):
                    e.wait_ge(squares, i * KC + k + 1)
                    last = e.matmul(ps[:, mean_bank(i), 0:T], mean_w, norm_a[:, k, :], start=(k == 0),
                                    stop=(k == KC - 1))
                if z == KC:
                    last.then_inc(mean_ready, 1)

            def index_scores(b, h):
                S = P * (b + 1)
                if h == 0:
                    if b == 0:
                        e.wait_ge(evac_v, evac[2][1])
                    else:
                        e.wait_ge(relu_ready, 4 * b)
                g, a = h % 4, h // 4
                rowg = slice(32 * g, 32 * g + 32)
                for z in range(2):
                    last = e.matmul(ps[:, 4 + g, 256 * a:256 * a + S], qi[rowg, a, z, P * b:P * b + P],
                                    ki[rowg, z, 0:S], start=(z == 0), stop=(z == 1))
                if h == 7:
                    last.then_inc(isc_ready, 1)

            def logits(b, h):
                S = P * (b + 1)
                if h == 0:
                    if b == 0:
                        e.wait_ge(evac_v, evac[9][1])
                        e.wait_ge(relu_ready, 8)
                    else:
                        e.wait_ge(probT_copied, 1)
                g, a = h % 4, h // 4
                rowg = slice(32 * g, 32 * g + 32)
                for z in range(2):
                    last = e.matmul(ps[:, 4 + g, 256 * a:256 * a + S], qa[rowg, a, z, P * b:P * b + P],
                                    ka[rowg, a, z, 0:S], start=(z == 0), stop=(z == 1))
                if h == 7:
                    last.then_inc(logit_ready, 1)

            def turn_probs(b):
                e.wait_ge(prob_ready, b + 1)
                for ck in range(b + 1):
                    for k in range(8):
                        last = e.transpose(ps[:, 4 + 2 * ck + k // 4, P * (k % 4):P * (k % 4) + P],
                                           prob[:, k, P * ck:P * ck + P], ident)
                last.then_inc(probT_ready, 1)

            def attend(b):
                e.wait_ge(probT_copied, (b + 1) * (b + 2) // 2)
                if b:
                    e.wait_ge(att_copied, b)
                for h in range(8):
                    k = 2 * (h % 4) + h // 4
                    out = ps[64 * (h % 2):64 * (h % 2) + 64, 3, P * (h // 2):P * (h // 2) + P]
                    for ck in range(b + 1):
                        last = e.matmul(out, va[:, ck, 64 * h:64 * h + 64], probT[:, ck, k, :],
                                        start=(ck == 0), stop=(ck == b))
                last.then_inc(att_ready, 1)

            def retention_scores(k):
                r, jc = k // 2, k % 2
                if r == 0 and jc == 0:
                    e.wait_ge(evac_v, evac[14][1])
                tile, rg = r // 2, slice(64 * (r % 2), 64 * (r % 2) + 64)
                first, width = ((0, 256), (256, 128))[jc]
                for z in range(2):
                    last = e.matmul(ps[:, 4 + r, first:first + width], kr[rg, tile, z, P * jc:P * jc + P],
                                    qr[rg, tile, z, P * jc:T], start=(z == 0), stop=(z == 1))
                if r == RET_H - 1 and jc:
                    last.then_inc(inner_ready, 1)

            def retain():
                e.wait_ge(inner_used, 1)
                e.wait_ge(evac_s, n_evac_s)
                for r in range(RET_H):
                    out = ps[:, 4 + r // 2, 256 * (r % 2):256 * (r % 2) + 256]
                    e.matmul(out, vr[:, 0, P * r:P * r + P], inner[:, r, 0:256], start=True, stop=False,
                             skip_group_check=True)
                    last = e.matmul(out[:, P:T], vr[:, 1, P * r:P * r + P], inner[:, r, 256:384], start=False,
                                    stop=True, skip_group_check=True)
                last.then_inc(ret_ready, 1)

            def group_mean():
                flat = ro.rearrange("p h t -> p (h t)")
                for c in range(2):
                    last = e.matmul(ps[:, 6 + c, :], mean_w, flat[:, 512 * c:512 * c + 512], start=True, stop=True)
                last.then_inc(gmean_ready, 1)

            def group_var():
                for r in range(RET_H):
                    last = e.matmul(ps[32 * r:32 * r + 32, 6, 0:T], mean_w[:, 0:32], rsq[:, r, :], start=True, stop=True)
                last.then_inc(gvar_ready, 1)

            def group_spread():
                for r in range(RET_H):
                    rows = slice(32 * r, 32 * r + 32)
                    last = e.matmul(ps[:, 4 + r, 0:T], mean_w[rows, :], rstd[rows, :],
                                    start=True, stop=True)
                last.then_inc(spread_ready, 1)

            e.wait_ge(kept_loaded, 16)
            e.wait_ge(c_silu, 1)
            for k in range(KC):
                last = e.matmul(ps[:, k // 4, P * (k % 4):P * (k % 4) + P], c_col[:, k:k + 1].to_broadcast([P, P]), ident,
                                start=True, stop=True)
            last.then_inc(c_spread, 1)
            mean_squares(0)
            e.wait_ge(c_ready, 1)

            first_blocks(0, [(proj_bank(s // 2)[:, 256 * (s % 2):256 * (s % 2) + 256], s % 2 == 0) for s in range(RING)],
                         lambda k: e.wait_ge(h_ready, k + 1), whole=True)
            for n in range(RING, N_IN):
                q = pair_of[n]
                kind, blocks = PAIRS[q][1:]
                if half_of[n] == 0 and q >= PROJ_BANKS:
                    e.wait_ge(*evac[q - PROJ_BANKS])
                among = None
                if n in INDEX_AMONG:
                    among = partial(index_scores, INDEX_AMONG.index(n))
                if n in LOGITS_AMONG:
                    among = partial(logits, LOGITS_AMONG.index(n))
                if n == INNER_AMONG:
                    among = retention_scores
                if kind != ROWS:
                    columns(n, n % RING, proj_bank(q)[:, 256 * half_of[n]:256 * half_of[n] + 256], among)
                elif half_of[n] == 0:
                    rows(n, blocks, proj_bank(q), among)
                for b in range(TH):
                    if n == PROBT_AFTER[b]:
                        turn_probs(b)
                    if n == ATT_AFTER[b]:
                        attend(b)
                if n == RET_AFTER:
                    retain()
            e.wait_ge(ret_copied, 1)
            group_mean()

            def mixed_chunk(k):
                if k == 0:
                    e.wait_ge(mix_ready, 1)
                if k == 2:
                    e.wait_ge(squared, 1)
                    e.wait_ge(centred, 1)
                    group_var()
                if k == 4:
                    e.wait_ge(gstd_ready, 1)
                    group_spread()
                if k >= 4:
                    e.wait_ge(mix_ready, k - 2)

            e.wait_ge(evac_v, n_evac_v - 1)
            e.wait_ge(gate_exp, 2)
            first_blocks(FIRST_OUT, [(ps[:, s, 0:T], True) for s in range(RING)], mixed_chunk)
            for c in range(RING, N_OUT):
                n = FIRST_OUT + c
                e.wait_ge(out_added, c - 3)
                columns(n, n % RING, ps[:, c % 4, 0:T])
                mean_squares(1, c - RING, c - RING + 1)
            mean_squares(1, RING, KC)
            e.wait_ge(out_added, KC)
            first_blocks(FIRST_PQ, [(ps[:, s, 0:T], True) for s in range(RING)],
                         lambda k: e.wait_ge(h_ready, KC + k + 1))
            def head_scores(h):
                e.wait_ge(qry_copied, 2 * h + 2)
                if h == 0:
                    e.wait_ge(sk_loaded, 16)
                if h >= 4:
                    e.wait_ge(score_copied, h - 3)
                for b in range(TH):
                    for w in range(2):
                        at = (2 * b + w) * P
                        last = e.matmul(ps[:, 4 + h % 4, at:at + P], qry[:, 2 * h + w, P * b:P * b + P],
                                        sk[:, 2 * h + w, :], start=True, stop=True)
                last.then_inc(score_ready, 1)

            for c in range(RING, N_PQ):
                e.wait_ge(qry_copied, c - 3)
                n = FIRST_PQ + c
                columns(n, n % RING, ps[:, c % 4, 0:T])
                if c % 2 == 0:
                    head_scores((c - RING) // 2)

            for j in range(RING):
                e.wait_ge(qry_copied, N_PQ - RING + j + 1)
                columns(FIRST_U + j, (FIRST_U + j) % RING, ps[:, j, 0:T])
                if j < 2:
                    head_scores(PEER_H - 2 + j)
            def expert_block(i, j):
                e.wait_ge(gelu_ready, i * RING + (j - RING + 1))
                columns(i * RING + (FIRST_U + j), (FIRST_U + j) % RING, ps[:, j, 0:T])

            n_first = (NKEYS - GROUPS) // RING
            with e.Fori(1, n_first) as i:
                for j in range(RING):
                    expert_block(i, j)

            def turn_picks():
                e.wait_ge(decoded, TH)
                for w in range(3):
                    for b in range(TH):
                        last = e.transpose(ps[:, 4 + w // 2, (w % 2) * T + P * b:(w % 2) * T + P * b + P],
                                           sel[:, w, P * b:P * b + P], ident)
                last.then_inc(sel_T, 1)

            def gate_rows(g, s, half, first=False):
                e.wait_ge(hot_ready, g + 1)
                if not first:
                    e.wait_ge(gates_used, g - 1)
                for t in range(GROUP):
                    for part in range(PARTS):
                        last = e.matmul(ps[:, s + (0 if half else 6), KEYS_H * t:KEYS_H * t + KEYS_H],
                                        hot_l[s][:, :, t], hot_r[s][:, part, :, t],
                                        start=(part == 0), stop=(part == PARTS - 1))
                last.then_inc(hot_used, 1)

            for j in range(RING):
                expert_block(n_first, j)
                if j == 1:
                    turn_picks()
            for g in range(RING - 1):
                gate_rows(g, g % 2, 0, first=g < 2)
            with e.Fori(1, GROUPS // RING) as i:
                for j in range(RING):
                    expert_block(i + n_first, j)
                    gate_rows(i * RING + (j - 1), (j - 1) % 2, 0)
            gate_rows(GROUPS - 1, 1, 0)
            e.wait_ge(gelu_ready, NKEYS - RING + 2)
            for g in range(2):
                gate_rows(GROUPS + g, g, 1)

            def mix_experts(i2, j, start, stop):
                slot = (FIRST_V + j) % RING
                e.wait_ge(wexp_lo, i2 + 1)
                e.wait_ge(lo_ready, i2 + (FIRST_V + 1))
                for c in range(KC):
                    last = product(ps[:, 4 + c // 2, (c % 2) * T:(c % 2) * T + T],
                                   (w_hi[slot][:, c, :], w_lo[slot][:, c, :]),
                                   (h_hi[:, j, :], h_lo[:, j, :]), start and c % 2 == 0, stop, check=False)
                last.then_inc(block_used, 1)

            for j in range(RING):
                mix_experts(j, j, j == 0, False)
                if j == 0:
                    for g in range(2, RING):
                        gate_rows(GROUPS + g, g % 2, 1)
                gate_rows(GROUPS + RING + j, j % 2, 1)
            with e.Fori(1, n_first - 1) as i:
                for j in range(RING):
                    mix_experts(i * RING + j, j, False, False)
                    gate_rows(i * RING + (GROUPS + RING + j), j % 2, 1)
            with e.Fori(n_first - 1, NKEYS // RING - 1) as i:
                for j in range(RING):
                    mix_experts(i * RING + j, j, False, False)
            for j in range(RING // 2):
                mix_experts(NKEYS - RING + j, j, False, False)
            e.wait_ge(wexp_lo, NKEYS)
            e.wait_ge(lo_ready, FIRST_V + NKEYS)
            for bank in range(KC // 2):
                for c in (2 * bank, 2 * bank + 1):
                    for j in range(RING // 2, RING):
                        slot = (FIRST_V + j) % RING
                        last = product(ps[:, 4 + bank, (c % 2) * T:(c % 2) * T + T],
                                       (w_hi[slot][:, c, :], w_lo[slot][:, c, :]), (h_hi[:, j, :], h_lo[:, j, :]),
                                       False, j == RING - 1, check=False)
                last.then_inc(mixed, 1)
                if bank > 1:
                    mean_squares(2, 2 * bank - 4, 2 * bank - 2)
            mean_squares(2, KC - 4, KC)


def _rope_tables():
    t = np.arange(T, dtype=np.float32)

    def cs(inv, copies):
        ang = t[None, :] * inv[:, None]
        c = np.tile(np.cos(ang), (copies, 1)).astype(np.float32)
        s = np.tile(np.sin(ang), (copies, 1)).astype(np.float32)
        return [c, s, s, c]

    att = (1.0 / (np.float32(10000.0) ** (np.arange(0, ATT_D, 2, dtype=np.float32) / ATT_D))).astype(np.float32)
    ret = (1.0 / (np.float32(10000.0) ** np.linspace(0.0, 1.0, RET_D // 2, dtype=np.float32))).astype(np.float32)
    log_g = np.log(1.0 - 2.0 ** (-5.0 - np.arange(RET_H, dtype=np.float64)))
    diff = np.arange(T)[None, :] - np.arange(P)[:, None]
    decay = [np.where(diff >= 0, np.exp(g * np.maximum(diff, 0)), 0.0) * RET_D ** -0.5 for g in log_g]
    causal = np.where(np.arange(P)[None, :] <= np.arange(P)[:, None], 0.0, NEG)
    tab = np.concatenate(cs(att, 4) + cs(ret, 2) + decay + [causal], axis=1).astype(np.float32)
    keep = np.stack([np.tile(np.arange(P), (P, 1)), np.eye(P), np.full((P, P), 1.0 / P)], axis=1).astype(np.float32)
    return np.ascontiguousarray(tab), np.ascontiguousarray(keep)


def _blocks(w):
    n = w.shape[1] // P
    return w.reshape(KC, P, n, P).transpose(2, 1, 0, 3).reshape(n, P, KC * P)


def _in_columns():
    at = dict(qa=0, ka=512, va=1024, qi=1536, ki=2048, wi=2112, qr=2120, kr=2632, vr=3144, gr=3656)
    out = []
    for name, kind, _ in PAIRS:
        base, i = at[name[:2]], int(name[2:] or 0)
        if name == "wi":
            out += [base + c for c in range(ATT_H)] + [-1] * (P - ATT_H)
        elif kind != ROT:
            out += range(base + 256 * i, base + 256 * i + 256)
        else:
            heads, half = (2, 64) if name[1] == "r" else (4, 32)
            for z in range(2):
                for g in range(heads):
                    head = 0 if name == "ki" else heads * i + g
                    out += [base + head * 2 * half + z * half + j for j in range(half)]
    return np.array(out)


def kernel(x, c, w_ada, b_ada, norm_mix_g, w_in, w_out, norm_ffn_g, w_pq, sub_keys, u_emb, v_emb, norm_final_g):
    import concourse.bacc as bacc
    from concourse.bass_utils import run_bass_kernel_spmd as run

    x, c, w_ada, b_ada, norm_mix_g, w_in, w_out, norm_ffn_g, w_pq, sub_keys, u_emb, v_emb, norm_final_g = (
        np.asarray(a) for a in (x, c, w_ada, b_ada, norm_mix_g, w_in, w_out, norm_ffn_g, w_pq, sub_keys,
                                u_emb, v_emb, norm_final_g))

    def columns(v):
        return v.reshape(-1, P).T

    tab, keep = _rope_tables()
    cols = _in_columns()
    w_cols = np.concatenate([w_in[0], np.zeros((D, 1), np.float32)], axis=1)[:, cols]
    arrays = {
        "xT": x[0].reshape(T, KC, P).transpose(2, 1, 0),
        "c_cols": columns(c[0]),
        "w_ada_first": np.concatenate([w_ada[0][:, z * D:z * D + D].T.reshape(KC, P, D) for z in range(2)], axis=2),
        "w_ada": w_ada[0][:, 2 * D:].T.reshape(-1, ADA_GROUP, P, D).transpose(0, 2, 1, 3).reshape(-1, P, ADA_GROUP * D),
        "b_ada": columns(b_ada[0]),
        "gains": np.stack([columns(norm_mix_g[0]), columns(norm_ffn_g[0]), columns(norm_final_g)], axis=1),
        "tables": tab,
        "keep": keep,
        "early": np.concatenate([_blocks(w_cols), _blocks(w_out[0]), _blocks(w_pq[0])]),
        "skeys": sub_keys[0].reshape(2 * PEER_H, NKEYS, P).transpose(2, 0, 1),
        "u": u_emb[0].reshape(NKEYS, NKEYS, KC, P).transpose(1, 3, 2, 0).reshape(NKEYS, P, KC * P),
        "v": v_emb[0].reshape(NKEYS, NKEYS, D).transpose(1, 0, 2),
    }
    nc = bacc.Bacc("TRN2", target_bir_lowering=False, num_devices=1)
    sent, args = {}, []
    for name, a in arrays.items():
        sent[name] = np.ascontiguousarray(a)
        args.append(nc.dram_tensor(name, a.shape, F32, kind="ExternalInput").ap())
    args.append(nc.dram_tensor("outT", (P, KC, T), F32, kind="ExternalOutput").ap())
    build(nc, *args)
    r = run(nc, [sent], core_ids=[0])
    y = np.asarray(r.results[0]["outT"])
    return np.ascontiguousarray(y.transpose(2, 1, 0).reshape(1, T, D))
```
